# Optimizing a Trainium2 kernel written in Bass

```python
import jax, jax.numpy as jnp
from jax import lax
import numpy as np

D_MODEL = 2048
BATCH = 1
SEQ = 256
DEPTH = 2

N_MIXERS = 2
NORM_EPS = 1e-6

ATT_HEADS = 16
ATT_HEAD_DIM = D_MODEL // ATT_HEADS
ATT_WIDTH = ATT_HEADS * ATT_HEAD_DIM
MOBA_BLOCK = 256
MOBA_TOPK = 3
MOBA_QCHUNK = 16
ROPE_THETA = 10000.0

MLSTM_HEADS = 8
MLSTM_V_WIDTH = 2 * D_MODEL
MLSTM_V_DIM = MLSTM_V_WIDTH // MLSTM_HEADS
MLSTM_QK_DIM = MLSTM_V_DIM // 2
MLSTM_QK_WIDTH = MLSTM_HEADS * MLSTM_QK_DIM
MLSTM_CONV = 4
MLSTM_CHUNK = 64
MLSTM_IN_WIDTH = 2 * MLSTM_QK_WIDTH + 3 * MLSTM_V_WIDTH + 2 * MLSTM_HEADS

kernel_name = "hybrid_moba_mlstm_adaln"

def rms_norm(x, w):
    xf = x.astype(jnp.float32)
    y = xf * lax.rsqrt(jnp.mean(xf * xf, axis=-1, keepdims=True) + NORM_EPS)
    return (y * w.astype(jnp.float32)).astype(x.dtype)

def rope(x):
    S, D = x.shape[1], x.shape[-1]
    half = D // 2
    inv = ROPE_THETA ** (-jnp.arange(half, dtype=jnp.float32) / half)
    ang = jnp.arange(S, dtype=jnp.float32)[:, None] * inv[None, :]
    cos = jnp.cos(ang)[None, :, None, :]
    sin = jnp.sin(ang)[None, :, None, :]
    xf = x.astype(jnp.float32)
    x1, x2 = xf[..., :half], xf[..., half:]
    return jnp.concatenate([x1 * cos - x2 * sin, x2 * cos + x1 * sin], axis=-1).astype(x.dtype)

def moba_attention(q, k, v):
    B, H, S, D = q.shape
    BS, QC = MOBA_BLOCK, MOBA_QCHUNK
    nb = -(-S // BS)
    pad = nb * BS - S
    kb = jnp.pad(k, ((0, 0), (0, 0), (0, pad), (0, 0))).reshape(B, H, nb, BS, D)
    vb = jnp.pad(v, ((0, 0), (0, 0), (0, pad), (0, 0))).reshape(B, H, nb, BS, D)
    k_mean = jnp.mean(kb.astype(jnp.float32), axis=3)
    q_blk = jnp.arange(S) // BS
    gate = jnp.einsum('bhsd,bhnd->bhsn', q.astype(jnp.float32), k_mean)
    past = jnp.arange(nb)[None, :] < q_blk[:, None]
    gate = jnp.where(past, gate, -jnp.inf)
    topk = min(MOBA_TOPK, nb)
    _, sel = lax.top_k(gate, topk)
    sel_ok = sel < q_blk[:, None]
    nq = S // QC
    scale = D ** -0.5

    def to_chunks(a):
        a = a.reshape(B, H, nq, QC, *a.shape[3:])
        return jnp.moveaxis(a, 2, 0)

    def chunk_fn(args):
        q_c, sel_c, ok_c, c_idx = args
        t0 = c_idx * QC
        blk = t0 // BS
        k_own = lax.dynamic_index_in_dim(kb, blk, axis=2, keepdims=False)
        v_own = lax.dynamic_index_in_dim(vb, blk, axis=2, keepdims=False)
        s_own = jnp.einsum('bhqd,bhkd->bhqk', q_c, k_own).astype(jnp.float32) * scale
        q_pos = t0 + jnp.arange(QC)
        k_pos = blk * BS + jnp.arange(BS)
        s_own = jnp.where(k_pos[None, :] <= q_pos[:, None], s_own, -jnp.inf)
        flat = sel_c.reshape(B, H, QC * topk)[:, :, :, None, None]
        k_sel = jnp.take_along_axis(kb, flat, axis=2).reshape(B, H, QC, topk, BS, D)
        v_sel = jnp.take_along_axis(vb, flat, axis=2).reshape(B, H, QC, topk, BS, D)
        s_sel = jnp.einsum('bhqd,bhqrkd->bhqrk', q_c, k_sel).astype(jnp.float32) * scale
        s_sel = jnp.where(ok_c[..., None], s_sel, -jnp.inf).reshape(B, H, QC, topk * BS)
        p = jax.nn.softmax(jnp.concatenate([s_own, s_sel], axis=-1), axis=-1)
        p_own = p[..., :BS].astype(v.dtype)
        p_sel = p[..., BS:].reshape(B, H, QC, topk, BS).astype(v.dtype)
        return (jnp.einsum('bhqk,bhkd->bhqd', p_own, v_own)
                + jnp.einsum('bhqrk,bhqrkd->bhqd', p_sel, v_sel))

    out = lax.map(chunk_fn, (to_chunks(q), to_chunks(sel), to_chunks(sel_ok), jnp.arange(nq)))
    return jnp.moveaxis(out, 0, 2).reshape(B, H, S, D)

def moba_branch(h, w_in, q_norm_w, k_norm_w, w_out):
    B, S, _ = h.shape
    proj = h @ w_in
    q, k, v, z = jnp.split(proj, 4, axis=-1)
    shp = (B, S, ATT_HEADS, ATT_HEAD_DIM)
    q = rope(rms_norm(q.reshape(shp), q_norm_w))
    k = rope(rms_norm(k.reshape(shp), k_norm_w))
    v = v.reshape(shp)
    o = moba_attention(q.transpose(0, 2, 1, 3), k.transpose(0, 2, 1, 3), v.transpose(0, 2, 1, 3))
    o = o.transpose(0, 2, 1, 3).reshape(B, S, ATT_WIDTH)
    return (o * jax.nn.silu(z)) @ w_out

def causal_depthwise_conv(x, w):
    K, C = w.shape
    return lax.conv_general_dilated(
        x, w[:, None, :].astype(x.dtype), window_strides=(1,), padding=[(K - 1, 0)],
        dimension_numbers=('NWC', 'WIO', 'NWC'), feature_group_count=C)

def mlstm_chunkwise(q, k, v, i_pre, f_pre):
    B, H, S, dk = q.shape
    dv = v.shape[-1]
    L = MLSTM_CHUNK
    nc = S // L
    q = q.astype(jnp.float32)
    k = k.astype(jnp.float32) * (dk ** -0.5)
    v = v.astype(jnp.float32)
    log_f = jax.nn.log_sigmoid(f_pre.astype(jnp.float32))
    i_pre = i_pre.astype(jnp.float32)

    def chunks(a):
        return jnp.moveaxis(a.reshape(B, H, nc, L, *a.shape[3:]), 2, 0)

    causal = jnp.tril(jnp.ones((L, L), dtype=bool))

    def step(carry, xs):
        C, n, m = carry
        qc, kc, vc, ic, lfc = xs
        b = jnp.cumsum(lfc, axis=-1)
        log_inter = b + m[..., None]
        log_D = b[..., :, None] - b[..., None, :] + ic[..., None, :]
        log_D = jnp.where(causal, log_D, -jnp.inf)
        m_t = jnp.maximum(log_inter, jnp.max(log_D, axis=-1))
        w_inter = jnp.exp(log_inter - m_t)
        s_qk = jnp.einsum('bhtd,bhsd->bhts', qc, kc) * jnp.exp(log_D - m_t[..., None])
        num = (w_inter[..., None] * jnp.einsum('bhtd,bhde->bhte', qc, C)
               + jnp.einsum('bhts,bhse->bhte', s_qk, vc))
        den = w_inter * jnp.einsum('bhtd,bhd->bht', qc, n) + jnp.sum(s_qk, axis=-1)
        h = num / jnp.maximum(jnp.abs(den), jnp.exp(-m_t))[..., None]
        b_L = b[..., -1]
        log_s = b_L[..., None] - b + ic
        m_new = jnp.maximum(b_L + m, jnp.max(log_s, axis=-1))
        decay = jnp.exp(b_L + m - m_new)
        ws = jnp.exp(log_s - m_new[..., None])
        C_new = decay[..., None, None] * C + jnp.einsum('bhs,bhsd,bhse->bhde', ws, kc, vc)
        n_new = decay[..., None] * n + jnp.einsum('bhs,bhsd->bhd', ws, kc)
        return (C_new, n_new, m_new), h

    init = (jnp.zeros((B, H, dk, dv), jnp.float32), jnp.zeros((B, H, dk), jnp.float32),
            jnp.zeros((B, H), jnp.float32))
    _, hs = lax.scan(step, init, (chunks(q), chunks(k), chunks(v), chunks(i_pre), chunks(log_f)))
    return jnp.moveaxis(hs, 0, 2).reshape(B, H, S, dv)

def mlstm_branch(h, w_in, gate_b, conv_w, norm_w, w_out):
    B, S, _ = h.shape
    H, dk, dv = MLSTM_HEADS, MLSTM_QK_DIM, MLSTM_V_DIM
    proj = h @ w_in
    o1 = 2 * MLSTM_QK_WIDTH
    o2 = o1 + MLSTM_V_WIDTH
    o3 = o2 + MLSTM_V_WIDTH
    o4 = o3 + MLSTM_V_WIDTH
    qk = jax.nn.silu(causal_depthwise_conv(proj[..., :o1], conv_w))
    q = qk[..., :MLSTM_QK_WIDTH].reshape(B, S, H, dk).transpose(0, 2, 1, 3)
    k = qk[..., MLSTM_QK_WIDTH:].reshape(B, S, H, dk).transpose(0, 2, 1, 3)
    v = proj[..., o1:o2].reshape(B, S, H, dv).transpose(0, 2, 1, 3)
    o_gate = jax.nn.sigmoid(proj[..., o2:o3])
    z = proj[..., o3:o4]
    gates = proj[..., o4:].astype(jnp.float32) + gate_b.astype(jnp.float32)
    i_pre = gates[..., :H].transpose(0, 2, 1)
    f_pre = gates[..., H:].transpose(0, 2, 1)
    hc = mlstm_chunkwise(q, k, v, i_pre, f_pre)
    hc = hc.transpose(0, 2, 1, 3).astype(h.dtype)
    hn = rms_norm(hc, norm_w.reshape(H, dv)).reshape(B, S, MLSTM_V_WIDTH)
    return (hn * o_gate * jax.nn.silu(z)) @ w_out

def setup_inputs(seed: int = 0) -> dict:
    key = jax.random.key(seed)
    ks = jax.random.split(key, 16)
    d = D_MODEL
    n_att = (DEPTH + 1) // 2
    n_ml = DEPTH // 2
    nrm = jax.random.normal
    x = nrm(ks[0], (BATCH, SEQ, d), jnp.float32)
    c = nrm(ks[1], (BATCH, d), jnp.float32)
    norm_w = 1.0 + 0.02 * nrm(ks[2], (DEPTH, d), jnp.float32)
    ada_w = nrm(ks[3], (DEPTH, d, 3 * d), jnp.float32) * d ** -0.5
    ada_b = 0.02 * nrm(ks[4], (DEPTH, 3 * d), jnp.float32)
    att_w_in = nrm(ks[5], (n_att, d, 4 * ATT_WIDTH), jnp.float32) * d ** -0.5
    att_q_norm = 1.0 + 0.02 * nrm(ks[6], (n_att, ATT_HEAD_DIM), jnp.float32)
    att_k_norm = 1.0 + 0.02 * nrm(ks[7], (n_att, ATT_HEAD_DIM), jnp.float32)
    att_w_out = nrm(ks[8], (n_att, ATT_WIDTH, d), jnp.float32) * ATT_WIDTH ** -0.5
    mlstm_w_in = nrm(ks[9], (n_ml, d, MLSTM_IN_WIDTH), jnp.float32) * d ** -0.5
    i_bias = 0.1 * nrm(ks[10], (n_ml, MLSTM_HEADS), jnp.float32)
    f_bias = 3.0 + 3.0 * jax.random.uniform(ks[11], (n_ml, MLSTM_HEADS), jnp.float32)
    mlstm_gate_b = jnp.concatenate([i_bias, f_bias], axis=-1)
    mlstm_conv_w = nrm(ks[12], (n_ml, MLSTM_CONV, 2 * MLSTM_QK_WIDTH), jnp.float32) * MLSTM_CONV ** -0.5
    mlstm_norm_w = 1.0 + 0.02 * nrm(ks[13], (n_ml, MLSTM_V_WIDTH), jnp.float32)
    mlstm_w_out = nrm(ks[14], (n_ml, MLSTM_V_WIDTH, d), jnp.float32) * MLSTM_V_WIDTH ** -0.5
    return {"x": x, "c": c, "norm_w": norm_w, "ada_w": ada_w, "ada_b": ada_b,
            "att_w_in": att_w_in, "att_q_norm": att_q_norm, "att_k_norm": att_k_norm,
            "att_w_out": att_w_out, "mlstm_w_in": mlstm_w_in, "mlstm_gate_b": mlstm_gate_b,
            "mlstm_conv_w": mlstm_conv_w, "mlstm_norm_w": mlstm_norm_w, "mlstm_w_out": mlstm_w_out}

def reference(x, c, norm_w, ada_w, ada_b, att_w_in, att_q_norm, att_k_norm, att_w_out,
              mlstm_w_in, mlstm_gate_b, mlstm_conv_w, mlstm_norm_w, mlstm_w_out):
    cond = jax.nn.silu(c)
    for layer in range(DEPTH):
        mod = cond @ ada_w[layer] + ada_b[layer]
        shift, scale, gate = jnp.split(mod, 3, axis=-1)
        h = rms_norm(x, norm_w[layer]) * (1.0 + scale[:, None, :]) + shift[:, None, :]
        j = layer // N_MIXERS
        if layer % N_MIXERS == 0:
            y = moba_branch(h, att_w_in[j], att_q_norm[j], att_k_norm[j], att_w_out[j])
        else:
            y = mlstm_branch(h, mlstm_w_in[j], mlstm_gate_b[j], mlstm_conv_w[j],
                             mlstm_norm_w[j], mlstm_w_out[j])
        x = x + gate[:, None, :] * y
    return x


_drawn_inputs = setup_inputs


def setup_inputs(seed=0):
    import zlib

    import numpy as np

    out = dict(_drawn_inputs(seed))
    spreads = {}
    factors = {'norm_w': 6.063, 'att_q_norm': 8.0, 'att_k_norm': 8.0, 'mlstm_norm_w': 8.0}
    for name, (base, spread) in spreads.items():
        noise = np.random.default_rng([zlib.crc32(name.encode()), seed]).standard_normal(out[name].shape)
        drawn = base * np.exp(spread * noise) if base else spread * noise
        out[name] = __import__('jax').numpy.asarray(drawn.astype(out[name].dtype))
    for name, factor in factors.items():
        out[name] = (out[name] * factor).astype(out[name].dtype)
    return out
```

```python
from contextlib import ExitStack

import concourse.bass as bass
from concourse import mybir

ALU = mybir.AluOpType
ACT = mybir.ActivationFunctionType
AX = mybir.AxisListType
F32 = mybir.dt.float32
F32R = mybir.dt.float32r
BF16 = mybir.dt.bfloat16

P = 128
D = 2048
SEQ = 256
NT = SEQ // P
KT = D // P
EPS = 1e-6

H0, HD = 16, 128
G0 = 4
HG = H0 // G0
H1, DK, DV = 8, 256, 512
QK1 = H1 * DK
VW1 = H1 * DV
TAPS = 4
SCALE0 = float(HD) ** -0.5
SCALE1 = float(DK) ** -0.5
MASKED = -1e36

NC = 512
KG = 2
UNIT = KT // KG
BODY = 5 * UNIT
HEAD = 4 * UNIT
LEAD = 5
NG0 = HEAD + (G0 - 1) * BODY + UNIT
NG = NG0 + HEAD + (H1 - 1) * BODY + UNIT
ADA_SLOTS = 4
CHUNKS = D // NC

C_ID, C_TRI, C_MASK, C_COS, C_SIN = 0, P, 3 * P, 4 * P, 4 * P + NT * HD
C_ALL = 4 * P + 2 * NT * HD


def build(nc, x, c, norm_w, ada_w, ada_b, att_w_in, att_q_norm, att_k_norm, att_w_out,
          mlstm_w_in, mlstm_gate_b, mlstm_conv_w, mlstm_norm_w, mlstm_w_out, consts, out):
    w_in0 = att_w_in[0].rearrange("(t p) n -> p t n", p=P)
    w_out0 = att_w_out[0].rearrange("(t p) n -> p t n", p=P)
    w_in1 = mlstm_w_in[0].rearrange("(t p) n -> p t n", p=P)
    w_out1 = mlstm_w_out[0].rearrange("(t p) n -> p t n", p=P)
    ada = [ada_w[l].rearrange("(t p) n -> p t n", p=P) for l in range(2)]
    x_v = x[0].rearrange("(t p) n -> p t n", p=P)
    out_v = out[0].rearrange("(t p) n -> p t n", p=P)

    ctx = ExitStack()
    with ctx:
        def sb(name, shape, dt=F32):
            return ctx.enter_context(nc.sbuf_tensor(name, shape, dt))

        raw = sb("raw", [P, LEAD, KG * NC])
        w_hi = sb("w_hi", [P, LEAD, KG * NC], F32R)
        w_lo = sb("w_lo", [P, LEAD, KG * NC], F32R)
        h_hi = sb("h_hi", [P, KT, SEQ], F32R)
        h_lo = sb("h_lo", [P, KT, SEQ], F32R)
        y_hi = sb("y_hi", [P, 4, SEQ], F32R)
        y_lo = sb("y_lo", [P, 4, SEQ], F32R)
        stream = sb("stream", [P, NT, D])
        ada_raw = sb("ada_raw", [P, ADA_SLOTS, KG, NC])
        ada_acc = sb("ada_acc", [P, 2, KG, NC])
        ada_bias = sb("ada_bias", [P, NC])
        gate = sb("gate", [P, D])
        scale_c = sb("scale_c", [P, 2, KT])
        shift_c = sb("shift_c", [P, 2, KT])
        cond = sb("cond", [P, KT])
        const = sb("const", [P, C_COS])
        mask_b = sb("mask_b", [P, P], BF16)
        ident_b = sb("ident_b", [P, P], BF16)
        ones = sb("ones", [P, P])
        neg_half = sb("neg_half", [P, 16])
        eps_c = sb("eps_c", [P, 16])
        per_hd = sb("per_hd", [P, 16])
        per_dv = sb("per_dv", [P, NT])
        norm_c = sb("norm_c", [P, 2 * KT])
        vnorm_c = sb("vnorm_c", [P, VW1 // P])
        conv_c = sb("conv_c", [P, 2 * QK1 // P, TAPS])
        rope_a = sb("rope_a", [P, 2, NT, HD])
        rope_b = sb("rope_b", [P, 2, NT, HD])
        gate_w = sb("gate_w", [P, KT, 2 * H1])
        gate_hi = sb("gate_hi", [P, KT, 2 * H1], F32R)
        gate_lo = sb("gate_lo", [P, KT, 2 * H1], F32R)
        gate_b = sb("gate_b", [P, 2 * H1])
        stat = sb("stat", [P, 112])
        work = sb("work", [P, 9728 + 4 * (SEQ + 3)])

        def part(a, n, pat=None, **kw):
            v = work[:, a:a + n]
            return v.rearrange(pat, **kw) if pat else v

        xn = part(0, 4096, "p (t n) -> p t n", t=NT)
        conv_rows = work[0:TAPS, 4096:8192]
        qk_norm = part(8192, 256, "p (s d) -> p s d", s=2)
        trig = part(8448, 512, "p (s t d) -> p s t d", s=2, t=NT)
        rows_c = work[0:KT, 8960:9088]
        rows_n = work[0:2 * KT, 9088:9216]
        rows_v = work[0:VW1 // P, 9216:9344]
        h_full = part(4096, 1024, "p (b n) -> p b n", b=2)
        qk_in = part(0, 2048, "p (s t h d) -> p s t h d", s=2, t=NT, h=HG)
        qkT = part(0, 2048, "p (h s t) -> p h s t", h=HG, s=2)
        rot = part(2048, 2048, "p (s t h d) -> p s t h d", s=2, t=NT, h=HG)
        pT0 = part(2048, 1536, "p (h n) -> p h n", h=HG)
        swapped = part(4096, 1024, "p (t h d) -> p t h d", t=NT, h=HG)
        v0 = part(5120, 1024, "p (t n) -> p t n", t=NT)
        z0 = part(6144, 1024, "p (t h d) -> p t h d", t=NT, h=HG)
        p0 = part(7168, 1536, "p (h n) -> p h n", h=HG)
        dump0 = part(7168, 1024, "p (t h d) -> p t h d", t=NT, h=HG)
        y0 = part(8704, 1024, "p (t n) -> p t n", t=NT)
        cv = part(0, 1024, "p (j t) -> p j t", j=4)
        v1 = part(1024, 1024, "p (t n) -> p t n", t=NT)
        o1 = part(2048, 1024, "p (t n) -> p t n", t=NT)
        z1 = part(3072, 1024, "p (t n) -> p t n", t=NT)
        y1 = part(4096, 1024, "p (t n) -> p t n", t=NT)
        decay = part(5120, 384)
        p1 = part(5504, 384)
        pT1 = part(5888, 384)
        a_bc = part(6272, H1 * 384, "p (h n) -> p h n", h=H1)
        qk_pad = part(9728, 4 * (SEQ + 3), "p (j t) -> p j t", j=4)
        g_pre = part(2048, 32, "p (t g) -> p t g", t=NT)
        g_a = part(2080, 16, "p (t g) -> p t g", t=NT)
        g_b = part(2096, 16, "p (t g) -> p t g", t=NT)
        log_f = part(2112, 16, "p (t g) -> p t g", t=NT)
        cum_f = work[0:H1, 3072:3328]
        a_row = work[0:H1, 3328:3584]
        m_row = work[0:H1, 3584:3840]
        m_tot = work[0:H1, 3840:4096]

        ident = const[:, C_ID:C_ID + P]
        tri = const[:, C_TRI:C_TRI + SEQ]
        xsq = stat[:, 0:8].rearrange("p (t c) -> p t c", t=NT)
        xss = stat[:, 8:10]
        xrs = stat[:, 10:12]
        qk_ss = stat[:, 12:28]
        qk_rs = stat[:, 28:44]
        row_max = stat[:, 44:52]
        q_scale = stat[:, 52:60]
        neg_max = stat[:, 60:68]
        row_sum = stat[:, 68:76]
        inv_sum = stat[:, 76:84]
        den1 = stat[:, 84:86]
        inv1 = stat[:, 86:88]
        ss1 = stat[:, 88:90]
        t1 = stat[:, 90:92]
        coef1 = stat[:, 92:94]
        neg_m = sb("neg_m", [P, NT, H1])
        floor_m = sb("floor_m", [P, NT, H1])

        a_bc_flat = part(6272, H1 * 384)
        scaled = ada_raw[:, 0]
        scale_flat = scale_c[:].rearrange("p l t -> p (l t)")
        shift_flat = shift_c[:].rearrange("p l t -> p (l t)")
        conv_flat = conv_c[:].rearrange("p j k -> p (j k)")
        neg_m_flat = neg_m[:].rearrange("p t h -> p (t h)")
        floor_flat = floor_m[:]
        BC_BANK = (0, 1, 3)

        proj = [[ctx.enter_context(nc.psum_tensor(f"proj{a}{t}", [P, NC], F32)) for t in range(NT)]
                for a in range(2)]
        mix = [ctx.enter_context(nc.psum_tensor(f"mix{i}", [P, NC], F32)) for i in range(4)]

        def sem(name):
            return ctx.enter_context(nc.semaphore(name))

        consts_in, rows_in, norms_in, gates_in = (sem(n) for n in (
            "consts_in", "rows_in", "norms_in", "gates_in"))
        x_in, x_again, ones_set, rows_turned = (sem(n) for n in (
            "x_in", "x_again", "ones_set", "rows_turned"))
        cond_ready, rows_out, masks_ready, rope_table = (sem(n) for n in (
            "cond_ready", "rows_out", "masks_ready", "rope_table"))
        pad_zeroed, half_set, hi_ready, lo_ready = (sem(n) for n in (
            "pad_zeroed", "half_set", "hi_ready", "lo_ready"))
        granule_used, ada_tile, ada_bias_in, ada_summed = (sem(n) for n in (
            "granule_used", "ada_tile", "ada_bias_in", "ada_summed"))
        gate_out, mod_out, bias_zeroed, in_evac = (sem(n) for n in (
            "gate_out", "mod_out", "bias_zeroed", "in_evac"))
        out_part, out_evac, xsq_ready, xss_ready = (sem(n) for n in (
            "out_part", "out_evac", "xsq_ready", "xss_ready"))
        xrs_step, xn_act, xn_dve, ht_done = (sem(n) for n in (
            "xrs_step", "xn_act", "xn_dve", "ht_done"))
        h_act, h_ready, rope_part, rope_done = (sem(n) for n in (
            "h_act", "h_ready", "rope_part", "rope_done"))
        qk_rs_step, qkt_done, qkT_ready, s0_done = (sem(n) for n in (
            "qk_rs_step", "qkt_done", "qkT_ready", "s0_done"))
        max_step, p0_ready, inv0_ready, pt0_done = (sem(n) for n in (
            "max_step", "p0_ready", "inv0_ready", "pt0_done"))
        pT0_ready, pv0_done, y_done, yt_done = (sem(n) for n in (
            "pT0_ready", "pv0_done", "y_done", "yt_done"))
        y_hi_ready, y_lo_ready, gate_hi_ready, gate_lo_ready = (sem(n) for n in (
            "y_hi_ready", "y_lo_ready", "gate_hi_ready", "gate_lo_ready"))
        gates_done, g_step, g_act, cum_done = (sem(n) for n in (
            "gates_done", "g_step", "g_act", "cum_done"))
        row_step, bc_done, bc_ready, m_done = (sem(n) for n in (
            "row_step", "bc_done", "bc_ready", "m_done"))
        neg_m_ready, floor_ready, conv_step, qk1_ready = (sem(n) for n in (
            "neg_m_ready", "floor_ready", "conv_step", "qk1_ready"))
        s1_done, d1_ready, p1_ready, den_step = (sem(n) for n in (
            "s1_done", "d1_ready", "p1_ready", "den_step"))
        pt1_done, pT1_ready, pv1_done, sq1_ready = (sem(n) for n in (
            "pt1_done", "pT1_ready", "pv1_done", "sq1_ready"))
        coef_step, y_part, x1_step, x1_chunk = (sem(n) for n in (
            "coef_step", "y_part", "x1_step", "x1_chunk"))
        stored, stream_zeroed = (sem(n) for n in (
            "stored", "stream_zeroed"))
        raw_in = [ctx.enter_context(nc.semaphore(f"raw_in{i}")) for i in range(LEAD)]
        ada_in = [ctx.enter_context(nc.semaphore(f"ada_in{i}")) for i in range(ADA_SLOTS)]

        def wait(eng, sem, value):
            if not isinstance(value, int) or value > 0:
                eng.wait_ge(sem, value)

        def number(it, c):
            return it * BODY + c

        def fills(it, c):
            return it * (BODY // LEAD) + (c // LEAD + 1)

        SHIFT, SCALE, GATE = 0, 1, 2
        ADA_START = [(0, SCALE if j % 2 == 0 else SHIFT, j // 2) for j in range(2 * CHUNKS)]
        ADA_GROUP = [(0, GATE), (1, SCALE), (1, SHIFT)]
        ADA_A = len(ADA_START) * UNIT
        ADA_G = len(ADA_GROUP) * UNIT
        ADA_L = ADA_A + G0 * ADA_G
        BLK_A, BLK_G = len(ADA_START), len(ADA_GROUP)
        BLK_L = BLK_A + G0 * BLK_G

        def ada_at(count, span):
            at = {}
            for a in range(count):
                at.setdefault(a * span // count, []).append(a)
            return at

        AT_HEAD0, AT_BODY0, AT_HEAD1 = ada_at(ADA_G, 27), ada_at(ADA_G, 35), ada_at(4 * UNIT, 27)

        SUM_HEAD0 = [(12, 3), (28, 3), (30, 2)]
        SUM_BODY0 = [(14, 3), (33, 2), (37, 3)]
        SUM_HEAD1 = [(8, 3), (16, 3), (22, 1), (28, 0)]

        def load_raw(sp, it, c, src, tiles=KG):
            wait(sp, lo_ready, number(it, c) - LEAD + 1)
            sp.dma_start(raw[:, c % LEAD, :].rearrange("p (t n) -> p t n", t=tiles), src
                         ).then_inc(raw_in[c % LEAD], 16)

        def load_in0(sp, g, it, c, i):
            u, t0 = i // UNIT, KG * (i % UNIT)
            load_raw(sp, it, c, w_in0[:, t0:t0 + KG, bass.ds(u * D + g * NC, NC)])

        def load_in1(sp, h, it, c, i):
            u, t0 = i // UNIT, KG * (i % UNIT)
            if u == 0:
                half, t0 = i // 4, 2 * KG * (i % 4)
                load_raw(sp, it, c, w_in1[:, t0:t0 + 2 * KG, bass.ds(h * DK + half * QK1, DK)], 2 * KG)
            else:
                load_raw(sp, it, c, w_in1[:, t0:t0 + KG, bass.ds(2 * QK1 + (u - 1) * VW1 + h * DV, NC)])

        def load_out(sp, w, g, it, c, q):
            t0 = KG * (q % 2)
            load_raw(sp, it, c, w[:, bass.ds(g * 4 + t0, KG), (q // 2) * NC:(q // 2 + 1) * NC])

        def load_ada(sp, layer, sec, b, it, first, a):
            n = first + a
            if a % UNIT == 0:
                wait(sp, ada_tile, it * (BLK_G * 16) + (n // UNIT * 16 - 15))
                sp.dma_start(ada_bias[0:1, :], ada_b[layer:layer + 1, bass.ds(b * NC + sec * D, NC)]
                             ).then_inc(ada_bias_in, 16)
            wait(sp, ada_tile, it * (ADA_G * KG) + (n - ADA_SLOTS + 1) * KG)
            t0 = KG * (a % UNIT)
            sp.dma_start(ada_raw[:, n % ADA_SLOTS], ada[layer][:, t0:t0 + KG, bass.ds(b * NC + sec * D, NC)]
                         ).then_inc(ada_in[n % ADA_SLOTS], 16)

        def sp_group0(sp, g, it, base, at, first, start, out_too):
            for i in range(BODY if out_too else HEAD):
                if i >= HEAD:
                    load_out(sp, w_out0, it, it, base + i, i - HEAD)
                elif i >= start:
                    load_in0(sp, g, it, base + i, i)
                for a in at.get(i - LEAD, []):
                    load_ada(sp, *ADA_GROUP[a // UNIT], g, it, first, a)

        def sp_program(sp):
            sp.dma_start(const[:], consts[:, 0:C_COS]).then_inc(consts_in, 16)
            sp.dma_start(rows_c, c[0].rearrange("(t p) -> t p", p=P)).then_inc(rows_in, 16)
            sp.dma_start(rows_n, norm_w.rearrange("l (t p) -> (l t) p", p=P)).then_inc(rows_in, 16)
            sp.dma_start(rows_v, mlstm_norm_w[0].rearrange("(t p) -> t p", p=P)).then_inc(rows_in, 16)
            sp.dma_start(conv_rows, mlstm_conv_w[0]).then_inc(rows_in, 16)
            sp.wait_ge(bias_zeroed, 1)
            for a in range(ADA_A):
                load_ada(sp, *ADA_START[a // UNIT], 0, 0, a)
                if a == 4:
                    sp.dma_start(stream[:], x_v).then_inc(x_in, 16)
                if a == 5:
                    sp.dma_start(trig, consts[:, C_COS:C_ALL].rearrange("p (s t d) -> p s t d", s=2, t=NT)
                                 ).then_inc(norms_in, 16)
                    for i, w in enumerate((att_q_norm, att_k_norm)):
                        sp.dma_start(qk_norm[:, i, :], w[0:1, :].to_broadcast([P, HD])).then_inc(norms_in, 16)
                    sp.dma_start(gate_b[:], mlstm_gate_b[0:1, :].to_broadcast([P, 2 * H1])
                                 ).then_inc(gates_in, 16)
                    sp.dma_start(gate_w[:], w_in1[:, :, 2 * QK1 + 3 * VW1:]).then_inc(gates_in, 16)
                if a >= ADA_A - LEAD:
                    load_in0(sp, 0, 0, a - ADA_A + LEAD, a - ADA_A + LEAD)
            sp_group0(sp, 0, 0, 0, AT_HEAD0, ADA_A, LEAD, False)
            with sp.Fori(0, G0 - 1) as it:
                sp_group0(sp, it + 1, it, HEAD, AT_BODY0, ADA_A + ADA_G, 0, True)
            base = HEAD + (G0 - 1) * BODY
            for q in range(UNIT):
                load_out(sp, w_out0, G0 - 1, 0, base + q, q)
            sp.wait_ge(ada_tile, KG * ADA_L)
            for q in range(CHUNKS):
                sp.dma_start(ada_raw[:, q], x_v[:, :, q * NC:(q + 1) * NC]).then_inc(x_again, 16)
            for i in range(HEAD):
                load_in1(sp, 0, 0, NG0 + i, i)
                for a in AT_HEAD1.get(i - LEAD, []):
                    if a == 0:
                        sp.wait_ge(x1_chunk, CHUNKS)
                    load_ada(sp, 1, GATE, a // UNIT, 0, ADA_L, a)
            with sp.Fori(0, H1 - 1) as it:
                for i in range(BODY):
                    if i < HEAD:
                        load_in1(sp, it + 1, it, NG0 + HEAD + i, i)
                    else:
                        load_out(sp, w_out1, it, it, NG0 + HEAD + i, i - HEAD)
            base = NG0 + HEAD + (H1 - 1) * BODY
            for q in range(UNIT):
                load_out(sp, w_out1, H1 - 1, 0, base + q, q)
            for q in range(CHUNKS):
                sp.wait_ge(out_evac, 2 + CHUNKS * (G0 + H1 - 1) + q + 1)
                sp.dma_start(out_v[:, :, q * NC:(q + 1) * NC], stream[:, :, q * NC:(q + 1) * NC]
                             ).then_inc(stored, 16)
            sp.wait_ge(stored, 16 * CHUNKS)

        def hi(act, it, c):
            act.wait_ge(raw_in[c % LEAD], fills(it, c) * 16)
            wait(act, granule_used, number(it, c) - LEAD + 1)
            act.activation(w_hi[:, c % LEAD, :], raw[:, c % LEAD, :], ACT.Copy).then_inc(hi_ready, 1)

        def norm_act(act, layer, first):
            for q in range(CHUNKS):
                if layer == 0:
                    act.wait_ge(x_in, 16)
                else:
                    act.wait_ge(x1_chunk, q + 1)
                for t in range(NT):
                    act.activation(xn[:, t, q * NC:(q + 1) * NC], stream[:, t, q * NC:(q + 1) * NC],
                                   ACT.Square, accum_out=xsq[:, t, q:q + 1]).then_inc(xsq_ready, 1)
            act.wait_ge(xrs_step, 2 * (layer + 1))
            for q in range(CHUNKS):
                act.activation(xn[:, 0, q * NC:(q + 1) * NC], stream[:, 0, q * NC:(q + 1) * NC],
                               ACT.Copy, scale=xrs[:, 0:1]).then_inc(xn_act, 1)
            for i in range(first):
                hi(act, 0, i)
            act.wait_ge(mod_out, 2 * CHUNKS * (layer + 1))
            for q in range(UNIT):
                act.wait_ge(ht_done, UNIT * layer + q + 1)
                wait(act, h_ready, UNIT * layer + q - 1)
                for k in range(2):
                    kt = 2 * q + k
                    ps = mix[q % 4][:, k * SEQ:(k + 1) * SEQ]
                    act.activation(h_hi[:, kt, :], ps, ACT.Identity, scale=scale_c[:, layer, kt:kt + 1],
                                   bias=shift_c[:, layer, kt:kt + 1])
                    act.activation(h_full[:, q % 2, k * SEQ:(k + 1) * SEQ], ps, ACT.Identity,
                                   scale=scale_c[:, layer, kt:kt + 1],
                                   bias=shift_c[:, layer, kt:kt + 1]).then_inc(h_act, 1)

        def q_evac(act, g, end):
            wait(act, s0_done, g)
            qk_evac(act, g, 0, end)

        def qk_evac(act, g, u, end):
            act.wait_ge(granule_used, end)
            for t in range(NT):
                act.activation(qk_in[:, u, t].rearrange("p h d -> p (h d)"), proj[u % 2][t][:], ACT.Copy)
            wait(act, in_evac, 4 * g + u)
            for t in range(NT):
                for h in range(HG):
                    i = (u * NT + t) * HG + h
                    op = act.activation(dump0[:, t, h], proj[u % 2][t][:, h * HD:(h + 1) * HD],
                                        ACT.Square, accum_out=qk_ss[:, i:i + 1])
            op.then_inc(in_evac, 1)

        def copy_evac(act, u, end, dst, func=ACT.Copy):
            act.wait_ge(granule_used, end)
            for t in range(NT):
                op = act.activation(dst[:, t, :], proj[u % 2][t][:], func)
            op.then_inc(in_evac, 1)

        def qkT_evac(act, g):
            act.wait_ge(qkt_done, g + 1)
            for h in range(HG):
                op = act.activation(qkT[:, h].rearrange("p s t -> p (s t)"), mix[h][:], ACT.Copy)
            op.then_inc(qkT_ready, 1)

        def exp0(act, g):
            act.wait_ge(max_step, 2 * g + 2)
            for h in range(HG):
                for t in range(NT):
                    a, b = (0, P) if t == 0 else (P, 3 * P)
                    i = t * HG + h
                    op = act.activation(p0[:, h, a:b], mix[h][:, a:b], ACT.Exp, scale=q_scale[:, i:i + 1],
                                        bias=neg_max[:, i:i + 1], accum_out=row_sum[:, i:i + 1])
            op.then_inc(p0_ready, 1)

        def pT0_evac(act, g):
            act.wait_ge(pt0_done, g + 1)
            for h in range(HG):
                op = act.activation(pT0[:, h, :], mix[h][:, 0:3 * P], ACT.Copy)
            op.then_inc(pT0_ready, 1)

        def y_hi_act(act, n, scales=None):
            act.wait_ge(yt_done, n + 1)
            for f in range(4):
                op = act.activation(y_hi[:, f, :], mix[2 + f // 2][:, (f % 2) * SEQ:(f % 2 + 1) * SEQ], ACT.Copy,
                                    **({} if scales is None else {"scale": vnorm_c[:, bass.ds(scales * 4 + f, 1)]}))
            op.then_inc(y_hi_ready, 1)

        def gate_evac(act, bank, k, b):
            act.wait_ge(ada_summed, k + 1)
            act.activation(gate[:, bass.ds(b * NC, NC)], mix[bank][:], ACT.Copy).then_inc(gate_out, 1)

        def act_group0(act, g, it, base):
            def end(u):
                return number(it, base + UNIT * (u + 1))
            tasks = {7: [lambda: q_evac(act, g, end(0))],
                     15: [lambda: qk_evac(act, g, 1, end(1))],
                     20: [lambda: qkT_evac(act, g)],
                     23: [lambda: copy_evac(act, 2, end(2), v0), lambda: exp0(act, g)],
                     27: [lambda: pT0_evac(act, g)],
                     31: [lambda: copy_evac(act, 3, end(3), z0.rearrange("p t h d -> p t (h d)"), ACT.Silu)]}
            return tasks

        def conv_in(act, h, end):
            act.wait_ge(granule_used, end)
            for b in range(2):
                op = act.activation(qk_pad[:, 2 * b:2 * b + 2, TAPS - 1:],
                                    proj[0][b][:].rearrange("p (j t) -> p j t", j=2), ACT.Copy)
            op.then_inc(in_evac, 1)

        def silu_qk(act, h):
            act.wait_ge(conv_step, 16 * h + 16)
            act.activation(cv.rearrange("p j t -> p (j t)"), cv.rearrange("p j t -> p (j t)"), ACT.Silu
                           ).then_inc(qk1_ready, 1)

        def decay1(act, h):
            if isinstance(h, int) and h == 0:
                act.wait_ge(neg_m_ready, 1)
                act.wait_ge(bc_ready, H1)
            for t in range(NT):
                a, b = (0, P) if t == 0 else (P, 3 * P)
                op = act.activation(decay[:, a:b], a_bc_flat[:, bass.ds(h * 384 + a, b - a)], ACT.Exp,
                                    bias=neg_m_flat[:, bass.ds(h + t * H1, 1)])
            op.then_inc(d1_ready, 1)

        def pT1_evac(act, h):
            act.wait_ge(pt1_done, h + 1)
            act.activation(pT1, mix[1][:, 0:3 * P], ACT.Copy).then_inc(pT1_ready, 1)

        def squares1(act, h):
            act.wait_ge(pv1_done, h + 1)
            for t in range(NT):
                op = act.activation(y1[:, t, :], mix[2 + t][:], ACT.Square, accum_out=ss1[:, t:t + 1])
            op.then_inc(sq1_ready, 1)

        def bc_evac(act, heads):
            for h in heads:
                act.wait_ge(bc_done, h + 1)
                act.activation(a_bc[:, h, :], mix[BC_BANK[h % 3]][:, 0:3 * P], ACT.Copy).then_inc(bc_ready, 1)

        def act_group1(act, h, it, base):
            def end(u):
                return number(it, base + UNIT * (u + 1))
            return {7: [lambda: conv_in(act, h, end(0))],
                    12: [lambda: silu_qk(act, h)],
                    14: [lambda: decay1(act, h)],
                    15: [lambda: copy_evac(act, 1, end(1), v1)],
                    17: [lambda: pT1_evac(act, h)],
                    19: [lambda: squares1(act, h)],
                    23: [lambda: copy_evac(act, 2, end(2), o1, ACT.Sigmoid)],
                    31: [lambda: copy_evac(act, 3, end(3), z1, ACT.Silu)]}

        def run(eng, prepare, it, base, n, tasks):
            for i in range(n):
                prepare(eng, it, base + i + LEAD)
                for task in tasks.get(i, []):
                    task()

        def merged(*tables):
            out = {}
            for t in tables:
                for i, tasks in t.items():
                    out.setdefault(i, []).extend(tasks)
            return out

        def act_program(act):
            act.wait_ge(consts_in, 16)
            act.activation(mask_b[:], const[:, C_MASK:C_MASK + P], ACT.Copy)
            act.activation(ident_b[:], ident, ACT.Copy).then_inc(masks_ready, 1)
            act.wait_ge(rows_turned, 1)
            act.activation(cond[:], proj[1][0][:, 0:KT], ACT.Silu).then_inc(cond_ready, 1)
            act.wait_ge(gates_in, 32)
            act.activation(gate_hi[:], gate_w[:], ACT.Copy).then_inc(gate_hi_ready, 1)
            norm_act(act, 0, LEAD)
            run(act, hi, 0, 0, HEAD, merged(
                act_group0(act, 0, 0, 0), {12: [lambda: gate_evac(act, 3, BLK_A, 0)]}))
            with act.Fori(0, G0 - 1) as it:
                run(act, hi, it, HEAD, BODY, merged(
                    {1: [lambda: y_hi_act(act, it)]}, act_group0(act, it + 1, it, HEAD),
                    {14: [lambda: gate_evac(act, 3, it * BLK_G + BLK_A + BLK_G, it + 1)]}))
            y_hi_act(act, G0 - 1)
            run(act, hi, 0, HEAD + (G0 - 1) * BODY, UNIT, {})
            norm_act(act, 1, 0)
            run(act, hi, 0, NG0, HEAD, merged(
                {8: [lambda: gates_exp(act)], 9: [lambda: gates_ln(act)],
                 11: [lambda: floor_exp(act), lambda: bc_evac(act, (0, 1, 2))],
                 12: [lambda: bc_evac(act, (3, 4, 5))], 13: [lambda: bc_evac(act, (6, 7))]},
                act_group1(act, 0, 0, NG0),
                {p: [lambda j=j, bank=bank: gate_evac(act, bank, BLK_L + j, j)]
                 for j, (p, bank) in enumerate(SUM_HEAD1)}))
            with act.Fori(0, H1 - 1) as it:
                run(act, hi, it, NG0 + HEAD, BODY, merged(
                    {1: [lambda: y_hi_act(act, it + G0, it)]}, act_group1(act, it + 1, it, NG0 + HEAD)))
            y_hi_act(act, G0 + H1 - 1, H1 - 1)
            base = NG0 + HEAD + (H1 - 1) * BODY
            run(act, hi, 0, base, UNIT - LEAD, {})

        def lo(dve, it, c):
            dve.wait_ge(hi_ready, number(it, c) + 1)
            dve.tensor_tensor(w_lo[:, c % LEAD, :], raw[:, c % LEAD, :], w_hi[:, c % LEAD, :].bitcast(F32),
                              ALU.subtract).then_inc(lo_ready, 1)

        def take_ada(dve, it, first, a, which):
            n = first + a
            dve.wait_ge(ada_in[n % ADA_SLOTS], it * (ADA_G // ADA_SLOTS * 16) + (n // ADA_SLOTS + 1) * 16)
            for k in range(KG):
                w, sum_ = ada_raw[:, n % ADA_SLOTS, k, :], ada_acc[:, which, k, :]
                t = KG * (a % UNIT) + k
                if a % UNIT:
                    dve.wait_ge(ada_tile, it * (ADA_G * KG) + (KG * n + k - 1))
                    op = dve.scalar_tensor_tensor(out=sum_, in0=w, scalar=cond[:, t:t + 1], in1=sum_,
                                                  op0=ALU.mult, op1=ALU.add)
                elif k == 0:
                    back = 0 if a == 0 and which == 0 else 1
                    wait(dve, ada_summed, it * BLK_G + (n // UNIT - back))
                    dve.wait_ge(ada_bias_in, it * (BLK_G * 16) + (n // UNIT + 1) * 16)
                    op = dve.scalar_tensor_tensor(out=sum_, in0=w, scalar=cond[:, t:t + 1], in1=ada_bias[:],
                                                  op0=ALU.mult, op1=ALU.add)
                else:
                    op = dve.tensor_scalar(sum_, w, cond[:, t:t + 1], None, ALU.mult)
                op.then_inc(ada_tile, 1)

        def ada_tasks(dve, it, first, at):
            return {i: [lambda a=a: take_ada(dve, it, first, a, (a // UNIT) % 2) for a in g] for i, g in at.items()}

        def mod_evac(dve, bank, k, layer, sec, b):
            dve.wait_ge(ada_summed, k + 1)
            src = mix[bank][:, 0:4]
            if sec == SCALE:
                op = dve.scalar_tensor_tensor(out=scale_flat[:, bass.ds(b * 4 + layer * KT, 4)], in0=src, scalar=1.0,
                                              in1=norm_c[:, bass.ds(b * 4 + layer * KT, 4)],
                                              op0=ALU.add, op1=ALU.mult)
            else:
                op = dve.tensor_copy(shift_flat[:, bass.ds(b * 4 + layer * KT, 4)], src)
            op.then_inc(mod_out, 1)

        def norm_sum(dve, layer):
            dve.wait_ge(xsq_ready, NT * CHUNKS * (layer + 1))
            dve.tensor_reduce(xss, xsq, AX.X, ALU.add).then_inc(xss_ready, 1)

        def norm_scale(dve, layer):
            dve.wait_ge(xrs_step, 2 * (layer + 1))
            for q in range(CHUNKS):
                dve.tensor_scalar(xn[:, 1, q * NC:(q + 1) * NC], stream[:, 1, q * NC:(q + 1) * NC],
                                  xrs[:, 1:2], None, ALU.mult).then_inc(xn_dve, 1)

        def norm_h(dve, layer):
            for q in range(UNIT):
                dve.wait_ge(h_act, KT * layer + 2 * (q + 1))
                dve.tensor_tensor(h_lo[:, 2 * q:2 * q + 2, :].rearrange("p k t -> p (k t)"), h_full[:, q % 2, :],
                                  h_hi[:, 2 * q:2 * q + 2, :].rearrange("p k t -> p (k t)").bitcast(F32),
                                  ALU.subtract).then_inc(h_ready, 1)

        def rope_tables(dve):
            dve.wait_ge(norms_in, 48)
            half = HD // 2
            for i in range(2):
                for t in range(NT):
                    dve.tensor_tensor(rope_a[:, i, t, :], trig[:, 0, t, :], qk_norm[:, i, :], ALU.mult)
                    dve.tensor_tensor(rope_b[:, i, t, 0:half], trig[:, 1, t, 0:half], qk_norm[:, i, half:HD], ALU.mult)
                    op = dve.tensor_tensor(rope_b[:, i, t, half:HD], trig[:, 1, t, half:HD], qk_norm[:, i, 0:half],
                                           ALU.mult)
            op.then_inc(rope_table, 1)

        def rope(dve, g, u):
            half = HD // 2
            dve.wait_ge(in_evac, 4 * g + u + 1)
            wait(dve, rope_done, 2 * g + u)
            if u == 0:
                wait(dve, pv0_done, g)
            src, dst = qk_in[:, u], rot[:, u]
            for t in range(NT):
                dve.tensor_tensor(dst[:, t], src[:, t], rope_a[:, u, t:t + 1, :].to_broadcast([P, HG, HD]), ALU.mult)
                dve.tensor_tensor(swapped[:, t, :, 0:half], src[:, t, :, half:HD],
                                  rope_b[:, u, t:t + 1, 0:half].to_broadcast([P, HG, half]), ALU.mult)
                op = dve.tensor_tensor(swapped[:, t, :, half:HD], src[:, t, :, 0:half],
                                       rope_b[:, u, t:t + 1, half:HD].to_broadcast([P, HG, half]), ALU.mult)
            op.then_inc(rope_part, 1)
            dve.wait_ge(rope_part, 3 * g + 1 + u)
            flat = "p t h d -> p (t h d)"
            op = dve.tensor_tensor(dst.rearrange(flat), dst.rearrange(flat), swapped.rearrange(flat), ALU.add)
            if u == 1:
                op.then_inc(rope_part, 1)
                dve.wait_ge(rope_part, 3 * g + 3)
                dve.wait_ge(qk_rs_step, 3 * g + 3)
                rs = qk_rs[:, 8:16].rearrange("p (n o) -> p n o", o=1).to_broadcast([P, 8, HD])
                op = dve.tensor_tensor(dst.rearrange("p t h d -> p (t h) d"), dst.rearrange("p t h d -> p (t h) d"),
                                       rs, ALU.mult)
            op.then_inc(rope_done, 1)

        def max0(dve, g):
            dve.wait_ge(s0_done, g + 1)
            for h in range(HG):
                for t in range(NT):
                    a, b = (0, P) if t == 0 else (P, 3 * P)
                    dve.reduce_max(row_max[:, t * HG + h:t * HG + h + 1], mix[h][:, a:b], AX.X)
            dve.tensor_scalar(q_scale, qk_rs[:, 0:8], SCALE0, None, ALU.mult).then_inc(max_step, 1)
            dve.wait_ge(max_step, 2 * g + 1)
            dve.scalar_tensor_tensor(out=neg_max, in0=row_max, scalar=-1.0, in1=q_scale,
                                     op0=ALU.mult, op1=ALU.mult).then_inc(max_step, 1)

        def inv0(dve, g):
            dve.wait_ge(p0_ready, g + 1)
            dve.reciprocal(inv_sum, row_sum).then_inc(inv0_ready, 1)

        def y0_out(dve, g):
            dve.wait_ge(pv0_done, g + 1)
            dve.wait_ge(inv0_ready, g + 1)
            dve.wait_ge(in_evac, 4 * g + 4)
            for t in range(NT):
                for h in range(HG):
                    i = t * HG + h
                    op = dve.scalar_tensor_tensor(out=y0[:, t, h * HD:(h + 1) * HD], in0=mix[t][:, h * HD:(h + 1) * HD],
                                                  scalar=inv_sum[:, i:i + 1], in1=z0[:, t, h], op0=ALU.mult,
                                                  op1=ALU.mult)
            op.then_inc(y_done, 1)

        def y_lo_dve(dve, n, scales=None):
            dve.wait_ge(y_hi_ready, n + 1)
            for f in range(4):
                src = mix[2 + f // 2][:, (f % 2) * SEQ:(f % 2 + 1) * SEQ]
                if scales is None:
                    op = dve.tensor_tensor(y_lo[:, f, :], src, y_hi[:, f, :].bitcast(F32), ALU.subtract)
                else:
                    op = dve.scalar_tensor_tensor(out=y_lo[:, f, :], in0=src, scalar=vnorm_c[:, bass.ds(scales * 4 + f, 1)],
                                                  in1=y_hi[:, f, :].bitcast(F32), op0=ALU.mult, op1=ALU.subtract)
            op.then_inc(y_lo_ready, 1)

        def out_evac0(dve, o, q, end):
            dve.wait_ge(granule_used, end)
            dve.wait_ge(out_evac, o * CHUNKS + (q + 2))
            for t in range(NT):
                x_t = stream[:, t, q * NC:(q + 1) * NC]
                op = dve.tensor_tensor(x_t, proj[q % 2][t][:], x_t, ALU.add)
            op.then_inc(out_evac, 1)

        def out_evac1(dve, o, q, end):
            dve.wait_ge(granule_used, end)
            dve.wait_ge(out_evac, o * CHUNKS + (q + 2))
            for t in range(NT):
                op = dve.tensor_tensor(scaled[:, t, :], proj[q % 2][t][:], gate[:, q * NC:(q + 1) * NC], ALU.mult)
            op.then_inc(out_part, 1)
            dve.wait_ge(out_part, (o - G0) * CHUNKS + (q + 1))
            for t in range(NT):
                x_t = stream[:, t, q * NC:(q + 1) * NC]
                op = dve.tensor_tensor(x_t, scaled[:, t, :], x_t, ALU.add)
            op.then_inc(out_evac, 1)

        def layer0_end(dve, q):
            dve.wait_ge(out_evac, 2 + CHUNKS * (G0 - 1) + q + 1)
            for t in range(NT):
                x_t = stream[:, t, q * NC:(q + 1) * NC]
                op = dve.tensor_tensor(x_t, x_t, gate[:, q * NC:(q + 1) * NC], ALU.mult)
            op.then_inc(x1_step, 1)
            dve.wait_ge(x1_step, q + 1)
            for t in range(NT):
                x_t = stream[:, t, q * NC:(q + 1) * NC]
                op = dve.tensor_tensor(x_t, x_t, ada_raw[:, q, t, :], ALU.add)
            op.then_inc(x1_chunk, 1)

        def conv(dve, h, tap):
            if tap == 0:
                dve.wait_ge(in_evac, 4 * h + 17)
            for j in range(4):
                w = conv_flat[:, bass.ds(h * (2 * TAPS) + ((j // 2) * (QK1 // P) + j % 2) * TAPS + tap, 1)]
                src = qk_pad[:, j, tap:tap + SEQ]
                if tap == 0:
                    op = dve.tensor_scalar(cv[:, j, :], src, w, None, ALU.mult)
                else:
                    dve.wait_ge(conv_step, h * 16 + (4 * tap + j - 3))
                    op = dve.scalar_tensor_tensor(out=cv[:, j, :], in0=src, scalar=w, in1=cv[:, j, :],
                                                  op0=ALU.mult, op1=ALU.add)
                op.then_inc(conv_step, 1)

        def p1_out(dve, h):
            dve.wait_ge(s1_done, h + 1)
            dve.wait_ge(d1_ready, h + 1)
            for t in range(NT):
                a, b = (0, P) if t == 0 else (P, 3 * P)
                op = dve.scalar_tensor_tensor(out=p1[:, a:b], in0=mix[0][:, a:b], scalar=SCALE1, in1=decay[:, a:b],
                                              op0=ALU.mult, op1=ALU.mult, accum_out=den1[:, t:t + 1])
            op.then_inc(p1_ready, 1)
            dve.wait_ge(p1_ready, h + 1)
            dve.scalar_tensor_tensor(out=inv1, in0=den1, scalar=-1.0, in1=den1, op0=ALU.mult, op1=ALU.max
                                     ).then_inc(den_step, 1)
            dve.wait_ge(den_step, 3 * h + 1)
            if isinstance(h, int) and h == 0:
                dve.wait_ge(floor_ready, 1)
            f = floor_flat[:, :, bass.ds(h, 1)]
            iv = inv1.rearrange("p (t o) -> p t o", o=1)
            dve.tensor_tensor(iv, iv, f, ALU.max).then_inc(den_step, 1)
            dve.wait_ge(den_step, 3 * h + 2)
            dve.reciprocal(inv1, inv1).then_inc(den_step, 1)

        def y1_part(dve, h):
            dve.wait_ge(coef_step, 6 * h + 6)
            dve.wait_ge(in_evac, 4 * h + 19)
            for t in range(NT):
                op = dve.scalar_tensor_tensor(out=y1[:, t, :], in0=mix[2 + t][:], scalar=coef1[:, t:t + 1],
                                              in1=o1[:, t, :], op0=ALU.mult, op1=ALU.mult)
            op.then_inc(y_part, 1)

        def y1_out(dve, h):
            dve.wait_ge(y_part, h + 1)
            dve.wait_ge(in_evac, 4 * h + 20)
            for t in range(NT):
                op = dve.tensor_tensor(y1[:, t, :], y1[:, t, :], z1[:, t, :], ALU.mult)
            op.then_inc(y_done, 1)

        def gates_exp(act):
            act.wait_ge(g_step, 3)
            act.activation(g_b, g_a, ACT.Exp).then_inc(g_act, 1)

        def gates_ln(act):
            act.wait_ge(g_step, 4)
            act.activation(g_a, g_b, ACT.Ln).then_inc(g_act, 1)

        def floor_exp(act):
            act.wait_ge(m_done, 1)
            act.activation(neg_m_flat, mix[2][:, 0:16], ACT.Copy, scale=-1.0).then_inc(neg_m_ready, 1)
            act.activation(floor_m[:].rearrange("p t h -> p (t h)"), mix[2][:, 16:32], ACT.Exp, scale=-1.0
                           ).then_inc(floor_ready, 1)

        def gates_a(dve):
            dve.wait_ge(gates_done, 1)
            for t in range(NT):
                op = dve.tensor_tensor(g_pre[:, t, :], mix[t][:, 0:2 * H1], gate_b[:], ALU.add)
            op.then_inc(g_step, 1)
            dve.wait_ge(g_step, 1)
            dve.tensor_scalar(g_a, g_pre[:, :, H1:], -1.0, None, ALU.mult).then_inc(g_step, 1)
            dve.wait_ge(g_step, 2)
            dve.tensor_tensor(g_a, g_a, g_pre[:, :, H1:], ALU.min).then_inc(g_step, 1)

        def gates_b(dve):
            dve.wait_ge(g_act, 1)
            dve.tensor_scalar(g_b, g_b, 1.0, None, ALU.add).then_inc(g_step, 1)

        def gates_c(dve):
            dve.wait_ge(g_act, 2)
            dve.tensor_scalar(log_f, g_pre[:, :, H1:], 0.0, None, ALU.min).then_inc(g_step, 1)
            dve.wait_ge(g_step, 5)
            dve.tensor_tensor(log_f, log_f, g_a, ALU.subtract).then_inc(g_step, 1)

        def gates_rows(dve):
            dve.wait_ge(cum_done, 1)
            dve.tensor_copy(cum_f, mix[0][0:H1, 0:SEQ]).then_inc(row_step, 1)
            dve.wait_ge(row_step, 1)
            dve.tensor_tensor(a_row, mix[1][0:H1, 0:SEQ], cum_f, ALU.subtract).then_inc(row_step, 1)
            dve.wait_ge(row_step, 2)
            dve.tensor_tensor_scan(out=m_row, data0=a_row, data1=a_row, initial=0.0, op0=ALU.max, op1=ALU.max
                                   ).then_inc(row_step, 1)
            dve.wait_ge(row_step, 3)
            dve.tensor_tensor(m_tot, cum_f, m_row, ALU.add).then_inc(row_step, 1)

        def dve_group0(dve, g, y_at):
            return {8: [lambda: rope(dve, g, 0)], 16: [lambda: rope(dve, g, 1)], 22: [lambda: max0(dve, g)],
                    25: [lambda: inv0(dve, g)], y_at: [lambda: y0_out(dve, g)]}

        def dve_group1(dve, h, y_at):
            return merged({8 + tap: [lambda tap=tap: conv(dve, h, tap)] for tap in range(TAPS)},
                          {14: [lambda: p1_out(dve, h)], 24: [lambda: y1_part(dve, h)], y_at: [lambda: y1_out(dve, h)]})

        def dve_program(dve):
            dve.wait_ge(rows_turned, 1)
            dve.tensor_copy(norm_c[:], proj[0][0][:, 32:64])
            dve.tensor_copy(vnorm_c[:], proj[0][0][:, 64:96])
            dve.tensor_copy(conv_flat, proj[0][1][:, 0:P]).then_inc(rows_out, 1)
            dve.wait_ge(rows_out, 1)
            dve.wait_ge(cond_ready, 1)
            for a in range(ADA_A):
                take_ada(dve, 0, 0, a, (a // UNIT) % 2)
                if a == UNIT:
                    rope_tables(dve)
                if a == 2 * UNIT:
                    dve.wait_ge(gate_hi_ready, 1)
                    dve.tensor_tensor(gate_lo[:], gate_w[:], gate_hi[:].bitcast(F32), ALU.subtract
                                      ).then_inc(gate_lo_ready, 1)
                if a == 12:
                    norm_sum(dve, 0)
                if a == 20:
                    norm_scale(dve, 0)
                if a % UNIT == 2 and a > UNIT:
                    k = a // UNIT - 1
                    mod_evac(dve, k % 4, k, *ADA_START[k])
            k = BLK_A - 1
            mod_evac(dve, k % 4, k, *ADA_START[k])
            for i in range(LEAD):
                lo(dve, 0, i)
            dve.wait_ge(rope_table, 1)
            norm_h(dve, 0)
            run(dve, lo, 0, 0, HEAD, merged(
                dve_group0(dve, 0, 31), ada_tasks(dve, 0, ADA_A, AT_HEAD0),
                {p: [lambda j=j, bank=bank: mod_evac(dve, bank, BLK_A + j, *ADA_GROUP[j], 0)]
                 for j, (p, bank) in enumerate(SUM_HEAD0) if j}))
            dve.wait_ge(stream_zeroed, 1)
            with dve.Fori(0, G0 - 1) as it:
                run(dve, lo, it, HEAD, BODY, merged(
                    {1: [lambda: y_lo_dve(dve, it)]}, dve_group0(dve, it + 1, 32),
                    {HEAD + 2 * q + 1: [lambda q=q: out_evac0(dve, it, q, number(it, HEAD + HEAD + 2 * q + 2))] for q in range(CHUNKS)},
                    ada_tasks(dve, it, ADA_A + ADA_G, AT_BODY0),
                    {p: [lambda j=j, bank=bank: mod_evac(dve, bank, it * BLK_G + BLK_A + BLK_G + j, *ADA_GROUP[j],
                                                         it + 1)]
                     for j, (p, bank) in enumerate(SUM_BODY0) if j}))
            y_lo_dve(dve, G0 - 1)
            dve.wait_ge(gate_out, CHUNKS)
            dve.wait_ge(x_again, 16 * CHUNKS)
            run(dve, lo, 0, HEAD + (G0 - 1) * BODY, UNIT, {
                2 * q + 1: [lambda q=q: out_evac0(dve, G0 - 1, q, HEAD + (G0 - 1) * BODY + 2 * q + 2), lambda q=q: layer0_end(dve, q)]
                for q in range(CHUNKS)})
            norm_sum(dve, 1)
            norm_scale(dve, 1)
            norm_h(dve, 1)
            dve.wait_ge(pad_zeroed, 1)
            run(dve, lo, 0, NG0, HEAD, merged(
                {7: [lambda: gates_a(dve)], 8: [lambda: gates_b(dve)], 9: [lambda: gates_c(dve)],
                 10: [lambda: gates_rows(dve)]},
                dve_group1(dve, 0, 31), ada_tasks(dve, 0, ADA_L, AT_HEAD1)))
            dve.wait_ge(gate_out, 2 * CHUNKS)
            with dve.Fori(0, H1 - 1) as it:
                run(dve, lo, it, NG0 + HEAD, BODY, merged(
                    {1: [lambda: y_lo_dve(dve, it + G0, it)]}, dve_group1(dve, it + 1, 32),
                    {HEAD + 2 * q + 1: [lambda q=q: out_evac1(dve, it + G0, q, number(it, NG0 + HEAD + HEAD + 2 * q + 2))] for q in range(CHUNKS)}))
            y_lo_dve(dve, G0 + H1 - 1, H1 - 1)
            base = NG0 + HEAD + (H1 - 1) * BODY
            for i in range(UNIT):
                if i < UNIT - LEAD:
                    lo(dve, 0, base + i + LEAD)
                if i % 2:
                    out_evac1(dve, G0 + H1 - 1, i // 2, base + i + 1)

        def gpsimd_program(pool):
            pool.memset(ada_bias[:], 0.0).then_inc(bias_zeroed, 1)
            pool.memset(ones[:], 1.0).then_inc(ones_set, 1)
            pool.memset(eps_c[:], EPS)
            pool.memset(per_hd[:], 1.0 / HD)
            pool.memset(per_dv[:], 1.0 / DV)
            pool.memset(neg_half[:], -0.5).then_inc(half_set, 1)
            pool.memset(qk_pad[:, :, 0:TAPS - 1], 0.0).then_inc(pad_zeroed, 1)
            pool.wait_ge(half_set, 1)

            def norm_power(layer):
                pool.wait_ge(xss_ready, layer + 1)
                pool.tensor_scalar(xrs, xss, 1.0 / D, EPS, ALU.mult, ALU.add).then_inc(xrs_step, 1)
                pool.wait_ge(xrs_step, 2 * layer + 1)
                pool.tensor_tensor(xrs, xrs, neg_half[:, 0:2], ALU.pow).then_inc(xrs_step, 1)

            norm_power(0)
            pool.wait_ge(xn_act, CHUNKS)
            pool.wait_ge(xn_dve, CHUNKS)
            pool.memset(stream[:, 0, :], 0.0)
            pool.memset(stream[:, 1, :], 0.0).then_inc(out_evac, 2)
            pool.wait_ge(out_evac, 2)
            pool.sem_inc(stream_zeroed, 1)
            with pool.Fori(0, G0) as g:
                pool.wait_ge(in_evac, 4 * g + 2)
                pool.tensor_tensor(qk_rs, qk_ss, per_hd[:], ALU.mult).then_inc(qk_rs_step, 1)
                pool.wait_ge(qk_rs_step, 3 * g + 1)
                pool.tensor_tensor(qk_rs, qk_rs, eps_c[:], ALU.add).then_inc(qk_rs_step, 1)
                pool.wait_ge(qk_rs_step, 3 * g + 2)
                pool.tensor_tensor(qk_rs, qk_rs, neg_half[:, 0:16], ALU.pow).then_inc(qk_rs_step, 1)
            norm_power(1)
            with pool.Fori(0, H1) as h:
                pool.wait_ge(sq1_ready, h + 1)
                pool.wait_ge(den_step, 3 * h + 3)
                pool.tensor_tensor(t1, inv1, inv1, ALU.mult).then_inc(coef_step, 1)
                for n, (operand, op) in enumerate(((ss1, ALU.mult), (per_dv[:], ALU.mult),
                                                   (eps_c[:, 0:NT], ALU.add), (neg_half[:, 0:NT], ALU.pow))):
                    pool.wait_ge(coef_step, 6 * h + (n + 1))
                    pool.tensor_tensor(t1, t1, operand, op).then_inc(coef_step, 1)
                pool.wait_ge(coef_step, 6 * h + 5)
                pool.tensor_tensor(coef1, t1, inv1, ALU.mult).then_inc(coef_step, 1)

        def slot(w, c, k):
            return w[:, c % LEAD, k * NC:(k + 1) * NC]

        def three(pe, out_, a_hi, a_lo, b_hi, b_lo, start, stop, **kw):
            pe.matmul(out_, a_hi, b_hi, start=start, stop=False, **kw)
            pe.matmul(out_, a_hi, b_lo, start=False, stop=False, **kw)
            return pe.matmul(out_, a_lo, b_hi, start=False, stop=stop, **kw)

        def unit_wait(pe, n, u, o):
            wait(pe, in_evac, n - 1)
            if u < 2 and not (isinstance(o, int) and o == 0):
                pe.wait_ge(out_evac, o * CHUNKS + (1 + u))

        def granule_in(pe, it, c, u, r, layer_first=None):
            pe.wait_ge(lo_ready, number(it, c) + 1)
            for k in range(KG):
                kt = KG * r + k
                for t in range(NT):
                    a, b = h_hi[:, kt, t * P:(t + 1) * P], h_lo[:, kt, t * P:(t + 1) * P]
                    op = three(pe, proj[u % 2][t][:], a, b, slot(w_hi, c, k), slot(w_lo, c, k),
                               kt == 0, kt == KT - 1)
            op.then_inc(granule_used, 1)

        def granule_qk1(pe, it, c, r):
            pe.wait_ge(lo_ready, number(it, c) + 1)
            for k in range(2 * KG):
                kt = 2 * KG * (r % 4) + k
                for j in range(2):
                    w = slice(k * DK + j * P, k * DK + (j + 1) * P)
                    op = three(pe, proj[0][r // 4][:, j * SEQ:(j + 1) * SEQ], w_hi[:, c % LEAD, w],
                               w_lo[:, c % LEAD, w], h_hi[:, kt, :], h_lo[:, kt, :],
                               kt == 0 and j == 0, kt == KT - 1, skip_group_check=True)
            op.then_inc(granule_used, 1)

        def granule_out(pe, o, it, c, q, n):
            j = q // 2
            pe.wait_ge(lo_ready, number(it, c) + 1)
            if q == 0:
                pe.wait_ge(y_lo_ready, o + 1)
            if q % 2 == 0:
                if j < 2:
                    pe.wait_ge(in_evac, n - 1 + j)
                else:
                    pe.wait_ge(out_evac, o * CHUNKS + (j + 1))
            for k in range(KG):
                f = KG * (q % 2) + k
                for t in range(NT):
                    a, b = y_hi[:, f, t * P:(t + 1) * P], y_lo[:, f, t * P:(t + 1) * P]
                    op = three(pe, proj[j % 2][t][:], a, b, slot(w_hi, c, k), slot(w_lo, c, k), f == 0, f == 3)
            op.then_inc(granule_used, 1)

        def turn_rows(pe):
            pe.wait_ge(consts_in, 16)
            pe.wait_ge(rows_in, 64)
            pe.transpose(proj[1][0][:, 0:KT], rows_c, ident[0:KT, 0:KT])
            pe.transpose(proj[0][0][:, 32:64], rows_n, ident[0:32, 0:32])
            pe.transpose(proj[0][0][:, 64:96], rows_v, ident[0:32, 0:32])
            for j in range(2 * QK1 // P):
                op = pe.transpose(proj[0][1][:, j * TAPS:(j + 1) * TAPS], conv_rows[:, j * P:(j + 1) * P],
                                  ident[0:TAPS, 0:TAPS])
            op.then_inc(rows_turned, 1)

        def turn_x(pe, layer, q):
            pe.wait_ge(xn_act, CHUNKS * layer + q // 2 + 1)
            pe.wait_ge(xn_dve, CHUNKS * layer + q // 2 + 1)
            if q >= 4:
                pe.wait_ge(h_act, KT * layer + 2 * (q - 3))
            for k in range(2):
                for t in range(NT):
                    kt = 2 * q + k
                    op = pe.transpose(mix[q % 4][:, k * SEQ + t * P:k * SEQ + (t + 1) * P],
                                      xn[:, t, kt * P:(kt + 1) * P], ident)
            op.then_inc(ht_done, 1)

        def ada_sum(pe, bank, k, which, sec):
            pe.wait_ge(ada_tile, k * 16 + 16)
            if sec == GATE:
                for i in range(KG):
                    op = pe.matmul(mix[bank][:], ones[:], ada_acc[:, which, i, :], start=(i == 0), stop=(i == KG - 1))
            else:
                for j in range(4):
                    for i in range(KG):
                        op = pe.matmul(mix[bank][:, j:j + 1], ada_acc[:, which, i, j * P:(j + 1) * P], ones[:, 0:1],
                                       start=(i == 0), stop=(i == KG - 1))
            op.then_inc(ada_summed, 1)

        def turn_qk0(pe, g):
            pe.wait_ge(rope_done, 2 * g + 2)
            wait(pe, y_lo_ready, g)
            pe.wait_ge(gate_out, g + 1)
            for h in range(HG):
                for u in range(2):
                    for t in range(NT):
                        op = pe.transpose(mix[h][:, (u * NT + t) * P:(u * NT + t + 1) * P], rot[:, u, t, h, :], ident)
            op.then_inc(qkt_done, 1)

        def masked(pe, bank):
            return pe.matmul(bank, ident_b[:], mask_b[:], start=False, stop=True)

        def scores0(pe, g):
            pe.wait_ge(qkT_ready, g + 1)
            for h in range(HG):
                q, k = qkT[:, h, 0, :], qkT[:, h, 1, :]
                pe.matmul(mix[h][:, 0:P], q[:, 0:P], k[:, 0:P], start=True, stop=False)
                masked(pe, mix[h][:, 0:P])
                pe.matmul(mix[h][:, P:3 * P], q[:, P:SEQ], k, start=True, stop=False, skip_group_check=True)
                op = pe.matmul(mix[h][:, 2 * P:3 * P], ident_b[:], mask_b[:], start=False, stop=True,
                               skip_group_check=True)
            op.then_inc(s0_done, 1)

        def turn_p0(pe, g):
            pe.wait_ge(p0_ready, g + 1)
            for h in range(HG):
                for i in range(3):
                    op = pe.transpose(mix[h][:, i * P:(i + 1) * P], p0[:, h, i * P:(i + 1) * P], ident)
            op.then_inc(pt0_done, 1)

        def pv0(pe, g):
            pe.wait_ge(pT0_ready, g + 1)
            pe.wait_ge(in_evac, 4 * g + 3)
            for h in range(HG):
                d = slice(h * HD, (h + 1) * HD)
                pe.matmul(mix[0][:, d], pT0[:, h, 0:P], v0[:, 0, d], start=True, stop=True)
                pe.matmul(mix[1][:, d], pT0[:, h, P:2 * P], v0[:, 0, d], start=True, stop=False)
                op = pe.matmul(mix[1][:, d], pT0[:, h, 2 * P:3 * P], v0[:, 1, d], start=False, stop=True)
            op.then_inc(pv0_done, 1)

        def turn_y(pe, n, y, mods=None):
            if mods is not None:
                pe.wait_ge(mod_out, mods)
            pe.wait_ge(y_done, n + 1)
            for f in range(4):
                for t in range(NT):
                    op = pe.transpose(mix[2 + f // 2][:, (f % 2) * SEQ + t * P:(f % 2) * SEQ + (t + 1) * P],
                                      y[:, t, f * P:(f + 1) * P], ident)
            op.then_inc(yt_done, 1)

        def pe_group0(pe, g):
            return {20: [lambda: turn_qk0(pe, g)], 22: [lambda: scores0(pe, g)], 27: [lambda: turn_p0(pe, g)],
                    31: [lambda: pv0(pe, g)]}

        def sum0(pe, j, g, *args):
            if j == 0:
                wait(pe, y_lo_ready, g)
            else:
                pe.wait_ge(pT0_ready, g + 1)
            ada_sum(pe, *args)

        def sums0(pe, g, it, places, first):
            return {p: [lambda j=j, bank=bank: sum0(pe, j, g, bank, it * BLK_G + (first + j), j % 2, ADA_GROUP[j][1])]
                    for j, (p, bank) in enumerate(places)}

        def gate1_sum(pe, j, bank):
            ada_sum(pe, bank, BLK_L + j, j % 2, GATE)

        def gates1(pe):
            pe.wait_ge(gate_lo_ready, 1)
            for t in range(NT):
                for kt in range(KT):
                    op = three(pe, mix[t][:, 0:2 * H1], h_hi[:, kt, t * P:(t + 1) * P], h_lo[:, kt, t * P:(t + 1) * P],
                               gate_hi[:, kt, :], gate_lo[:, kt, :], kt == 0, kt == KT - 1)
            op.then_inc(gates_done, 1)

        def gates_cum(pe):
            pe.wait_ge(g_step, 6)
            pe.matmul(mix[0][0:H1, 0:SEQ], log_f[:, 0, :], tri[:, 0:SEQ], start=True, stop=False,
                      skip_group_check=True)
            pe.matmul(mix[0][0:H1, P:SEQ], log_f[:, 1, :], tri[:, 0:P], start=False, stop=True,
                      skip_group_check=True)
            for t in range(NT):
                op = pe.transpose(mix[1][0:H1, t * P:(t + 1) * P], g_pre[:, t, 0:H1], ident)
            op.then_inc(cum_done, 1)

        def turn_m(pe):
            pe.wait_ge(row_step, 4)
            for i, row in enumerate((m_row, m_tot)):
                for t in range(NT):
                    op = pe.transpose(mix[2][:, (i * NT + t) * H1:(i * NT + t + 1) * H1],
                                      row[:, t * P:(t + 1) * P], ident[0:H1, 0:H1])
            op.then_inc(m_done, 1)

        def broadcast_a(pe, heads, before):
            wait(pe, bc_ready, before)
            for h in heads:
                bank = mix[BC_BANK[h % 3]]
                if h == 2:
                    pe.wait_ge(gate_out, CHUNKS + 1)
                one = ident[0:H1, h:h + 1].to_broadcast([H1, P])
                pe.matmul(bank[:, 0:P], one, a_row[:, 0:P], start=True, stop=False)
                masked(pe, bank[:, 0:P])
                pe.matmul(bank[:, P:3 * P], one, a_row, start=True, stop=False, skip_group_check=True)
                pe.matmul(bank[:, 2 * P:3 * P], ident_b[:], mask_b[:], start=False, stop=True,
                          skip_group_check=True).then_inc(bc_done, 1)

        def scores1(pe, h):
            pe.wait_ge(qk1_ready, h + 1)
            if isinstance(h, int):
                pe.wait_ge(bc_ready, H1)
            else:
                pe.wait_ge(p1_ready, h)
            for a, b, q in ((0, P, slice(0, P)), (P, 3 * P, slice(P, SEQ))):
                for j in range(2):
                    op = pe.matmul(mix[0][:, a:b], cv[:, j, q], cv[:, 2 + j, 0:b - a], start=(j == 0), stop=(j == 1))
            op.then_inc(s1_done, 1)

        def turn_p1(pe, h):
            pe.wait_ge(p1_ready, h + 1)
            for i in range(3):
                op = pe.transpose(mix[1][:, i * P:(i + 1) * P], p1[:, i * P:(i + 1) * P], ident)
            op.then_inc(pt1_done, 1)

        def pv1(pe, h):
            pe.wait_ge(pT1_ready, h + 1)
            pe.wait_ge(in_evac, 4 * h + 18)
            pe.wait_ge(y_lo_ready, h + G0)
            if isinstance(h, int):
                pe.wait_ge(gate_out, CHUNKS + 2)
            pe.matmul(mix[2][:], pT1[:, 0:P], v1[:, 0, :], start=True, stop=True)
            pe.matmul(mix[3][:], pT1[:, P:2 * P], v1[:, 0, :], start=True, stop=False)
            pe.matmul(mix[3][:], pT1[:, 2 * P:3 * P], v1[:, 1, :], start=False, stop=True).then_inc(pv1_done, 1)

        def pe_group1(pe, h):
            return {14: [lambda: scores1(pe, h)], 17: [lambda: turn_p1(pe, h)], 19: [lambda: pv1(pe, h)]}

        def pe_segment(pe, it, base, layer, group, o, tasks, out_too, start=None):
            for i in range(BODY if out_too else HEAD):
                u, r = i // UNIT, i % UNIT
                if u < 4 and r == 0:
                    unit_wait(pe, group * 4 + (4 * G0 * layer + u), u, o)
                if start and u == 0:
                    start(i)
                if u == 4:
                    granule_out(pe, o, it, base + i, r, group * 4 + (4 * G0 * layer + 4))
                elif u == 0 and layer == 1:
                    granule_qk1(pe, it, base + i, r)
                else:
                    granule_in(pe, it, base + i, u, r)
                for task in tasks.get(i, []):
                    task()

        def pe_program(pe):
            turn_rows(pe)
            pe.wait_ge(ones_set, 1)
            for k in range(BLK_A):
                wait(pe, mod_out, k - 3)
                ada_sum(pe, k % 4, k, k % 2, ADA_START[k][1])
            pe.wait_ge(mod_out, BLK_A)
            pe.wait_ge(rows_out, 1)
            pe.wait_ge(masks_ready, 1)

            def start(layer):
                turned = {0: {i: [i + 4] for i in range(4)}, 1: {1: [4, 5], 2: [6, 7]}}[layer]

                def step(i):
                    for q in turned.get(i, []):
                        turn_x(pe, layer, q)
                    need = i + 1 if layer == 0 else min(UNIT, 2 * (i + 1))
                    pe.wait_ge(h_ready, UNIT * layer + need)
                return step

            for q in range(4):
                turn_x(pe, 0, q)
            pe_segment(pe, 0, 0, 0, 0, 0, merged(
                pe_group0(pe, 0), sums0(pe, 0, 0, SUM_HEAD0, BLK_A)), False, start(0))
            with pe.Fori(0, G0 - 1) as it:
                pe_segment(pe, it, HEAD, 0, it + 1, it, merged(
                    {1: [lambda: turn_y(pe, it, y0, 2 * it + (BLK_A + 2))]}, pe_group0(pe, it + 1),
                    sums0(pe, it + 1, it, SUM_BODY0, BLK_A + BLK_G)), True)
            turn_y(pe, G0 - 1, y0, BLK_A + 2 * G0)
            for q in range(UNIT):
                granule_out(pe, G0 - 1, 0, HEAD + (G0 - 1) * BODY + q, q, 4 * G0)
            pe.wait_ge(mod_out, BLK_A + 2 * G0)
            pe.wait_ge(y_lo_ready, G0)
            for q in range(4):
                turn_x(pe, 1, q)
            pe_segment(pe, 0, NG0, 1, 0, G0, merged(
                {7: [lambda: gates1(pe)], 10: [lambda: gates_cum(pe)],
                 11: [lambda: turn_m(pe), lambda: broadcast_a(pe, (0, 1, 2), 0)],
                 12: [lambda: broadcast_a(pe, (3, 4, 5), 3)], 13: [lambda: broadcast_a(pe, (6, 7), 6)]},
                pe_group1(pe, 0),
                {p: [lambda j=j, bank=bank: gate1_sum(pe, j, bank)] for j, (p, bank) in enumerate(SUM_HEAD1)}),
                False, start(1))
            pe.wait_ge(gate_out, 2 * CHUNKS)
            with pe.Fori(0, H1 - 1) as it:
                pe_segment(pe, it, NG0 + HEAD, 1, it + 1, it + G0, merged(
                    {1: [lambda: turn_y(pe, it + G0, y1)]}, pe_group1(pe, it + 1)), True)
            turn_y(pe, G0 + H1 - 1, y1)
            for q in range(UNIT):
                granule_out(pe, G0 + H1 - 1, 0, NG0 + HEAD + (H1 - 1) * BODY + q, q, 4 * (G0 + H1))

        block = ctx.enter_context(nc.Block())

        @block.sync
        def _(sp):
            sp_program(sp)

        @block.scalar
        def _(act):
            act_program(act)

        @block.vector
        def _(dve):
            dve_program(dve)

        @block.gpsimd
        def _(pool):
            gpsimd_program(pool)

        @block.tensor
        def _(pe):
            pe_program(pe)


_INS = ["x", "c", "norm_w", "ada_w", "ada_b", "att_w_in", "att_q_norm", "att_k_norm", "att_w_out",
        "mlstm_w_in", "mlstm_gate_b", "mlstm_conv_w", "mlstm_norm_w", "mlstm_w_out"]


def _constants():
    import numpy as np
    out = np.zeros((P, C_ALL), np.float32)
    out[:, C_ID:C_ID + P] = np.eye(P)
    out[:, C_TRI:C_TRI + P] = np.triu(np.ones((P, P)))
    out[:, C_TRI + P:C_TRI + 2 * P] = 1.0
    out[:, C_MASK:C_MASK + P] = np.triu(np.full((P, P), MASKED), 1)
    half = HD // 2
    inv = np.float32(10000.0) ** (-np.arange(half, dtype=np.float32) / np.float32(half))
    ang = np.arange(SEQ, dtype=np.float32)[:, None] * inv[None, :]
    cos, sin = np.cos(ang), np.sin(ang)
    for t in range(NT):
        rows = slice(t * P, (t + 1) * P)
        out[:, C_COS + t * HD:C_COS + (t + 1) * HD] = np.concatenate([cos[rows], cos[rows]], 1)
        out[:, C_SIN + t * HD:C_SIN + (t + 1) * HD] = np.concatenate([-sin[rows], sin[rows]], 1)
    return out


def kernel(**inputs):
    import numpy as np
    import concourse.bacc as bacc
    from concourse.bass_utils import run_bass_kernel_spmd

    nc = bacc.Bacc("TRN2", target_bir_lowering=False, num_devices=1)
    arrays = {f"in_{n}": np.ascontiguousarray(inputs[n]) for n in _INS}
    arrays["in_consts"] = _constants()
    args = [nc.dram_tensor(n, a.shape, mybir.dt.from_np(a.dtype), kind="ExternalInput").ap()
            for n, a in arrays.items()]
    out = nc.dram_tensor("out_0", (1, SEQ, D), F32, kind="ExternalOutput").ap()
    build(nc, *args, out)
    r = run_bass_kernel_spmd(nc, [arrays], core_ids=[0])
    return r.results[0]["out_0"]
```

```python
from contextlib import ExitStack

import concourse.bass as bass
from concourse import mybir

ALU = mybir.AluOpType
ACT = mybir.ActivationFunctionType
AX = mybir.AxisListType
F32 = mybir.dt.float32
F32R = mybir.dt.float32r
BF16 = mybir.dt.bfloat16

P = 128
D = 2048
SEQ = 256
NT = SEQ // P
KT = D // P
EPS = 1e-6

H0, HD = 16, 128
G0 = 4
HG = H0 // G0
H1, DK, DV = 8, 256, 512
QK1 = H1 * DK
VW1 = H1 * DV
TAPS = 4
SCALE0 = float(HD) ** -0.5
SCALE1 = float(DK) ** -0.5
MASKED = -1e36

NC = 512
KG = 2
UNIT = KT // KG
BODY = 5 * UNIT
HEAD = 4 * UNIT
LEAD = 5
NG0 = HEAD + (G0 - 1) * BODY + UNIT
NG = NG0 + HEAD + (H1 - 1) * BODY + UNIT
ADA_SLOTS = 4
CHUNKS = D // NC

C_ID, C_TRI, C_MASK, C_COS, C_SIN = 0, P, 3 * P, 4 * P, 4 * P + NT * HD
C_ALL = 4 * P + 2 * NT * HD


def build(nc, x, c, norm_w, ada_w, ada_b, att_w_in, att_q_norm, att_k_norm, att_w_out,
          mlstm_w_in, mlstm_gate_b, mlstm_conv_w, mlstm_norm_w, mlstm_w_out, consts, out):
    w_in0 = att_w_in[0].rearrange("(t p) n -> p t n", p=P)
    w_out0 = att_w_out[0].rearrange("(t p) n -> p t n", p=P)
    w_in1 = mlstm_w_in[0].rearrange("(t p) n -> p t n", p=P)
    w_out1 = mlstm_w_out[0].rearrange("(t p) n -> p t n", p=P)
    ada = [ada_w[l].rearrange("(t p) (s n) -> p t s n", p=P, n=D) for l in range(2)]
    ada_rows = ada_b.rearrange("l (s n) -> l s n", n=D)
    x_v = x[0].rearrange("(t p) n -> p t n", p=P)
    out_v = out[0].rearrange("(t p) n -> p t n", p=P)

    ctx = ExitStack()
    with ctx:
        def sb(name, shape, dt=F32):
            return ctx.enter_context(nc.sbuf_tensor(name, shape, dt))

        raw = sb("raw", [P, LEAD, KG * NC])
        w_hi = sb("w_hi", [P, LEAD, KG * NC], F32R)
        w_lo = sb("w_lo", [P, LEAD, KG * NC], F32R)
        h_hi = sb("h_hi", [P, KT, SEQ], F32R)
        h_lo = sb("h_lo", [P, KT, SEQ], F32R)
        y_hi = sb("y_hi", [P, 4, SEQ], F32R)
        y_lo = sb("y_lo", [P, 4, SEQ], F32R)
        stream = sb("stream", [P, NT, D])
        ada_raw = sb("ada_raw", [P, ADA_SLOTS, 2, NC])
        ada_acc = sb("ada_acc", [P, 2, 2, NC])
        ada_bias = sb("ada_bias", [P, 2, NC])
        gate = sb("gate", [P, D])
        scale_c = sb("scale_c", [P, 2, KT])
        shift_c = sb("shift_c", [P, 2, KT])
        cond = sb("cond", [P, KT])
        const = sb("const", [P, C_COS])
        mask_b = sb("mask_b", [P, P], BF16)
        ident_b = sb("ident_b", [P, P], BF16)
        ones = sb("ones", [P, P])
        neg_half = sb("neg_half", [P, 16])
        eps_c = sb("eps_c", [P, 16])
        per_hd = sb("per_hd", [P, 16])
        per_dv = sb("per_dv", [P, NT])
        norm_c = sb("norm_c", [P, 2 * KT])
        vnorm_c = sb("vnorm_c", [P, VW1 // P])
        conv_c = sb("conv_c", [P, 2 * QK1 // P, TAPS])
        rope_a = sb("rope_a", [P, 2, NT, HD])
        rope_b = sb("rope_b", [P, 2, NT, HD])
        gate_w = sb("gate_w", [P, KT, 2 * H1])
        gate_hi = sb("gate_hi", [P, KT, 2 * H1], F32R)
        gate_lo = sb("gate_lo", [P, KT, 2 * H1], F32R)
        gate_b = sb("gate_b", [P, 2 * H1])
        stat = sb("stat", [P, 112])
        work = sb("work", [P, 9728 + 4 * (SEQ + 3)])

        def part(a, n, pat=None, **kw):
            v = work[:, a:a + n]
            return v.rearrange(pat, **kw) if pat else v

        xn = part(0, 4096, "p (t n) -> p t n", t=NT)
        conv_rows = work[0:TAPS, 4096:8192]
        qk_norm = part(8192, 256, "p (s d) -> p s d", s=2)
        trig = part(8448, 512, "p (s t d) -> p s t d", s=2, t=NT)
        rows_c = work[0:KT, 8960:9088]
        rows_n = work[0:2 * KT, 9088:9216]
        rows_v = work[0:VW1 // P, 9216:9344]
        h_full = part(4096, 1024, "p (b n) -> p b n", b=2)
        qk_in = part(0, 2048, "p (s t h d) -> p s t h d", s=2, t=NT, h=HG)
        qkT = part(0, 2048, "p (h s t) -> p h s t", h=HG, s=2)
        rot = part(2048, 2048, "p (s t h d) -> p s t h d", s=2, t=NT, h=HG)
        pT0 = part(2048, 1536, "p (h n) -> p h n", h=HG)
        swapped = part(4096, 1024, "p (t h d) -> p t h d", t=NT, h=HG)
        v0 = part(5120, 1024, "p (t n) -> p t n", t=NT)
        z0 = part(6144, 1024, "p (t h d) -> p t h d", t=NT, h=HG)
        p0 = part(7168, 1536, "p (h n) -> p h n", h=HG)
        dump0 = part(7168, 1024, "p (t h d) -> p t h d", t=NT, h=HG)
        y0 = part(8704, 1024, "p (t n) -> p t n", t=NT)
        cv = part(0, 1024, "p (j t) -> p j t", j=4)
        v1 = part(1024, 1024, "p (t n) -> p t n", t=NT)
        o1 = part(2048, 1024, "p (t n) -> p t n", t=NT)
        z1 = part(3072, 1024, "p (t n) -> p t n", t=NT)
        y1 = part(4096, 1024, "p (t n) -> p t n", t=NT)
        decay = part(5120, 384)
        p1 = part(5504, 384)
        pT1 = part(5888, 384)
        a_bc = part(6272, H1 * 384, "p (h n) -> p h n", h=H1)
        qk_pad = part(9728, 4 * (SEQ + 3), "p (j t) -> p j t", j=4)
        g_pre = part(2048, 32, "p (t g) -> p t g", t=NT)
        g_a = part(2080, 16, "p (t g) -> p t g", t=NT)
        g_b = part(2096, 16, "p (t g) -> p t g", t=NT)
        log_f = part(2112, 16, "p (t g) -> p t g", t=NT)
        cum_f = work[0:H1, 3072:3328]
        a_row = work[0:H1, 3328:3584]
        m_row = work[0:H1, 3584:3840]
        m_tot = work[0:H1, 3840:4096]

        ident = const[:, C_ID:C_ID + P]
        tri = const[:, C_TRI:C_TRI + SEQ]
        xsq = stat[:, 0:8].rearrange("p (t c) -> p t c", t=NT)
        xss = stat[:, 8:10]
        xrs = stat[:, 10:12]
        qk_ss = stat[:, 12:28]
        qk_rs = stat[:, 28:44]
        row_max = stat[:, 44:52]
        q_scale = stat[:, 52:60]
        neg_max = stat[:, 60:68]
        row_sum = stat[:, 68:76]
        inv_sum = stat[:, 76:84]
        den1 = stat[:, 84:86]
        inv1 = stat[:, 86:88]
        ss1 = stat[:, 88:90]
        t1 = stat[:, 90:92]
        coef1 = stat[:, 92:94]
        neg_m = sb("neg_m", [P, NT, H1])
        floor_m = sb("floor_m", [P, NT, H1])

        a_bc_flat = part(6272, H1 * 384)
        y_hi_last, y_lo_last = h_hi[:, 0:4, :], h_lo[:, 0:4, :]
        scaled = ada_raw[:, 0]
        scale_flat = scale_c[:].rearrange("p l t -> p (l t)")
        shift_flat = shift_c[:].rearrange("p l t -> p (l t)")
        conv_flat = conv_c[:].rearrange("p j k -> p (j k)")
        neg_m_flat = neg_m[:].rearrange("p t h -> p (t h)")
        floor_flat = floor_m[:]
        BC_BANK = (0, 1, 3)

        proj = [[ctx.enter_context(nc.psum_tensor(f"proj{a}{t}", [P, NC], F32)) for t in range(NT)]
                for a in range(2)]
        mix = [ctx.enter_context(nc.psum_tensor(f"mix{i}", [P, NC], F32)) for i in range(4)]

        def sem(name):
            return ctx.enter_context(nc.semaphore(name))

        consts_in, rows_in, norms_in, gates_in = (sem(n) for n in (
            "consts_in", "rows_in", "norms_in", "gates_in"))
        x_in, x_again, ones_set, rows_turned = (sem(n) for n in (
            "x_in", "x_again", "ones_set", "rows_turned"))
        cond_ready, rows_out, masks_ready, rope_table = (sem(n) for n in (
            "cond_ready", "rows_out", "masks_ready", "rope_table"))
        pad_zeroed, half_set, hi_ready, lo_ready = (sem(n) for n in (
            "pad_zeroed", "half_set", "hi_ready", "lo_ready"))
        granule_used, ada_tile, ada_bias_in, ada_summed = (sem(n) for n in (
            "granule_used", "ada_tile", "ada_bias_in", "ada_summed"))
        gate_out, mod_out, bias_zeroed, in_evac = (sem(n) for n in (
            "gate_out", "mod_out", "bias_zeroed", "in_evac"))
        out_part, out_evac, xsq_ready, xss_ready = (sem(n) for n in (
            "out_part", "out_evac", "xsq_ready", "xss_ready"))
        xrs_step, xn_act, xn_dve, ht_done = (sem(n) for n in (
            "xrs_step", "xn_act", "xn_dve", "ht_done"))
        h_act, h_ready, rope_part, rope_done = (sem(n) for n in (
            "h_act", "h_ready", "rope_part", "rope_done"))
        qk_rs_step, qkt_done, qkT_ready, s0_done = (sem(n) for n in (
            "qk_rs_step", "qkt_done", "qkT_ready", "s0_done"))
        max_step, p0_ready, inv0_ready, pt0_done = (sem(n) for n in (
            "max_step", "p0_ready", "inv0_ready", "pt0_done"))
        pT0_ready, pv0_done, y_done, yt_done = (sem(n) for n in (
            "pT0_ready", "pv0_done", "y_done", "yt_done"))
        y_hi_ready, y_lo_ready, gate_hi_ready, gate_lo_ready = (sem(n) for n in (
            "y_hi_ready", "y_lo_ready", "gate_hi_ready", "gate_lo_ready"))
        gates_done, g_step, g_act, cum_done = (sem(n) for n in (
            "gates_done", "g_step", "g_act", "cum_done"))
        row_step, bc_done, bc_ready, m_done = (sem(n) for n in (
            "row_step", "bc_done", "bc_ready", "m_done"))
        neg_m_ready, floor_ready, conv_step, qk1_ready = (sem(n) for n in (
            "neg_m_ready", "floor_ready", "conv_step", "qk1_ready"))
        s1_done, d1_ready, p1_ready, den_step = (sem(n) for n in (
            "s1_done", "d1_ready", "p1_ready", "den_step"))
        pt1_done, pT1_ready, pv1_done, sq1_ready = (sem(n) for n in (
            "pt1_done", "pT1_ready", "pv1_done", "sq1_ready"))
        coef_step, y_part, x1_step, x1_chunk = (sem(n) for n in (
            "coef_step", "y_part", "x1_step", "x1_chunk"))
        stored, stream_zeroed, gate_summed = (sem(n) for n in (
            "stored", "stream_zeroed", "gate_summed"))
        raw_in = [ctx.enter_context(nc.semaphore(f"raw_in{i}")) for i in range(LEAD)]
        ada_in = [ctx.enter_context(nc.semaphore(f"ada_in{i}")) for i in range(ADA_SLOTS)]

        def wait(eng, sem, value):
            if not isinstance(value, int) or value > 0:
                eng.wait_ge(sem, value)

        def number(it, c):
            return it * BODY + c

        def fills(it, c):
            return it * (BODY // LEAD) + (c // LEAD + 1)

        MOD, GATE = 0, 1
        ADA_LOOP = 4 * KT
        ADA_GATE0 = ADA_LOOP + (G0 - 2) * 2 * KT
        ADA_GATE1 = ADA_GATE0 + 2 * KT

        def ada_at(count, span):
            at = {}
            for a in range(count):
                at.setdefault(a * span // count, []).append(a)
            return at

        def two_blocks(first, second):
            return {p + a: [n * KT + a] for n, p in enumerate((first, second)) for a in range(KT)}

        AT_LOOP = two_blocks(0, 19)
        AT_GATE0 = two_blocks(0, 17)
        AT_GATE1 = ada_at(2 * KT, 27)

        MIXED = 3 * UNIT

        def head0(i):
            if i >= MIXED:
                return 3, i - MIXED
            block, j = i // 6, i % 6
            return (j // 2, 2 * block + j % 2) if block == 3 else (j % 3, 2 * block + j // 3)

        H_STEPS = (2, 3)
        LO_STEPS = (5, 6, 8, 9, 10, 12)

        def mixed_at(b, a):
            steps = LO_STEPS if b else range(KT - 6, KT)
            return [i for j, i in enumerate(range(6 * b - 1, 6 * b + 5)) if steps[j] == a and 0 <= i < MIXED]

        SUM_LOOP = [(18, 3), (36, 3)]
        SUM_GATE0 = [(18, 3), (19, 2), (36, 3), (37, 2)]
        SUM_GATE1 = [(16, 3), (17, 3), (28, 0), (29, 1)]

        def load_raw(sp, it, c, src, tiles=KG):
            wait(sp, lo_ready, number(it, c) - LEAD + 1)
            sp.dma_start(raw[:, c % LEAD, :].rearrange("p (t n) -> p t n", t=tiles), src
                         ).then_inc(raw_in[c % LEAD], 16)

        def load_in0(sp, g, it, c, i):
            u, t0 = i // UNIT, KG * (i % UNIT)
            load_raw(sp, it, c, w_in0[:, t0:t0 + KG, bass.ds(u * D + g * NC, NC)])

        def load_in1(sp, h, it, c, i):
            u, t0 = i // UNIT, KG * (i % UNIT)
            if u == 0:
                half, t0 = i // 4, 2 * KG * (i % 4)
                load_raw(sp, it, c, w_in1[:, t0:t0 + 2 * KG, bass.ds(h * DK + half * QK1, DK)], 2 * KG)
            else:
                load_raw(sp, it, c, w_in1[:, t0:t0 + KG, bass.ds(2 * QK1 + (u - 1) * VW1 + h * DV, NC)])

        def load_out(sp, w, g, it, c, q):
            t0 = KG * (q % 2)
            load_raw(sp, it, c, w[:, bass.ds(g * 4 + t0, KG), (q // 2) * NC:(q // 2 + 1) * NC])

        def load_ada(sp, layer, kind, b, it, first, a):
            n = first + a
            cols = [slice(0, 2), bass.ds(b * NC, NC)] if kind == MOD else [slice(2, 3), bass.ds(b * 2 * NC, 2 * NC)]
            if a % KT == 0:
                wait(sp, ada_tile, it * (2 * KT) + (n - KT + 1))
                bias = ada_bias[0:1] if kind == MOD else ada_bias[0:1].rearrange("p s n -> p (s n)")
                sp.dma_start(bias, ada_rows[layer:layer + 1, cols[0], cols[1]]).then_inc(ada_bias_in, 16)
            wait(sp, ada_tile, it * (2 * KT) + (n - ADA_SLOTS + 1))
            dst = ada_raw[:, n % ADA_SLOTS]
            if kind == GATE:
                dst = dst.rearrange("p s n -> p (s n)")
            sp.dma_start(dst, ada[layer][:, a % KT, cols[0], cols[1]]).then_inc(ada_in[n % ADA_SLOTS], 16)

        def sp_group0(sp, it, ada_granule, at):
            for i in range(BODY):
                if i < HEAD:
                    load_in0(sp, it + 1, it, HEAD + i, i)
                else:
                    load_out(sp, w_out0, it, it, HEAD + i, i - HEAD)
                for a in at.get(i - LEAD, []):
                    ada_granule(a)

        def sp_group1(sp, it):
            for i in range(BODY):
                if i < HEAD:
                    load_in1(sp, it + 1, it, NG0 + HEAD + i, i)
                else:
                    load_out(sp, w_out1, it, it, NG0 + HEAD + i, i - HEAD)

        def sp_program(sp):
            sp.dma_start(const[:], consts[:, 0:C_COS]).then_inc(consts_in, 16)
            sp.dma_start(rows_c, c[0].rearrange("(t p) -> t p", p=P)).then_inc(rows_in, 16)
            sp.dma_start(rows_n, norm_w.rearrange("l (t p) -> (l t) p", p=P)).then_inc(rows_in, 16)
            sp.dma_start(rows_v, mlstm_norm_w[0].rearrange("(t p) -> t p", p=P)).then_inc(rows_in, 16)
            sp.dma_start(conv_rows, mlstm_conv_w[0]).then_inc(rows_in, 16)
            sp.wait_ge(bias_zeroed, 1)

            def mixed_granule(i):
                u, r = head0(i)
                load_in0(sp, 0, 0, i, u * UNIT + r)

            for b in range(4):
                for a in range(KT):
                    load_ada(sp, 0, MOD, b, 0, b * KT, a)
                    if b == 0 and a == 4:
                        sp.dma_start(stream[:], x_v).then_inc(x_in, 16)
                    for i in mixed_at(b, a + 1):
                        mixed_granule(i)
                if b == 0:
                    sp.dma_start(trig, consts[:, C_COS:C_ALL].rearrange("p (s t d) -> p s t d", s=2, t=NT)
                                 ).then_inc(norms_in, 16)
                    for i, w in enumerate((att_q_norm, att_k_norm)):
                        sp.dma_start(qk_norm[:, i, :], w[0:1, :].to_broadcast([P, HD])).then_inc(norms_in, 16)
            mixed_granule(MIXED - 1)
            for i in range(MIXED, HEAD):
                load_in0(sp, 0, 0, i, i)
            sp.dma_start(gate_b[:], mlstm_gate_b[0:1, :].to_broadcast([P, 2 * H1])).then_inc(gates_in, 16)
            sp.dma_start(gate_w[:], w_in1[:, :, 2 * QK1 + 3 * VW1:]).then_inc(gates_in, 16)
            with sp.Fori(0, G0 - 2) as it:
                sp_group0(sp, it, lambda a: load_ada(sp, 1, MOD, it * 2 + a // KT, it, ADA_LOOP, a), AT_LOOP)
            sp_group0(sp, G0 - 2, lambda a: load_ada(sp, 0, GATE, a // KT, 0, ADA_GATE0, a), AT_GATE0)
            base = HEAD + (G0 - 1) * BODY
            for q in range(UNIT):
                load_out(sp, w_out0, G0 - 1, 0, base + q, q)
            sp.wait_ge(ada_tile, ADA_GATE1)
            for q in range(CHUNKS):
                sp.dma_start(ada_raw[:, q], x_v[:, :, q * NC:(q + 1) * NC]).then_inc(x_again, 16)
            for i in range(HEAD):
                load_in1(sp, 0, 0, NG0 + i, i)
                for a in AT_GATE1.get(i - LEAD, []):
                    if a == 0:
                        sp.wait_ge(x1_chunk, CHUNKS)
                    load_ada(sp, 1, GATE, a // KT, 0, ADA_GATE1, a)
            with sp.Fori(0, H1 - 2) as it:
                sp_group1(sp, it)
            sp_group1(sp, H1 - 2)
            base = NG0 + HEAD + (H1 - 1) * BODY
            for q in range(UNIT):
                load_out(sp, w_out1, H1 - 1, 0, base + q, q)
            for q in range(CHUNKS):
                sp.wait_ge(out_evac, 2 + CHUNKS * (G0 + H1 - 1) + q + 1)
                sp.dma_start(out_v[:, :, q * NC:(q + 1) * NC], stream[:, :, q * NC:(q + 1) * NC]
                             ).then_inc(stored, 16)
            sp.wait_ge(stored, 16 * CHUNKS)

        def hi(act, it, c):
            act.wait_ge(raw_in[c % LEAD], fills(it, c) * 16)
            wait(act, granule_used, number(it, c) - LEAD + 1)
            act.activation(w_hi[:, c % LEAD, :], raw[:, c % LEAD, :], ACT.Copy).then_inc(hi_ready, 1)

        def norm_act(act, layer):
            for q in range(CHUNKS):
                if layer == 0:
                    act.wait_ge(x_in, 16)
                else:
                    act.wait_ge(x1_chunk, q + 1)
                for t in range(NT):
                    act.activation(xn[:, t, q * NC:(q + 1) * NC], stream[:, t, q * NC:(q + 1) * NC],
                                   ACT.Square, accum_out=xsq[:, t, q:q + 1]).then_inc(xsq_ready, 1)
            act.wait_ge(xrs_step, 2 * (layer + 1))
            for q in range(CHUNKS):
                if layer == 1 and q > 1:
                    h_make(act, 1, 2 * (q - 2))
                    h_make(act, 1, 2 * (q - 2) + 1)
                act.activation(xn[:, 0, q * NC:(q + 1) * NC], stream[:, 0, q * NC:(q + 1) * NC],
                               ACT.Copy, scale=xrs[:, 0:1]).then_inc(xn_act, 1)

        def turn_bank(layer, q):
            return mix[q % 4] if layer else mix[3 - q % 2]

        def h_make(act, layer, q):
            act.wait_ge(mod_out, q // 2 + 1 if layer == 0 else 2 * CHUNKS)
            act.wait_ge(ht_done, UNIT * layer + q + 1)
            wait(act, h_ready, UNIT * layer + q - 1)
            for k in range(2):
                kt = 2 * q + k
                ps = turn_bank(layer, q)[:, k * SEQ:(k + 1) * SEQ]
                act.activation(h_hi[:, kt, :], ps, ACT.Identity, scale=scale_c[:, layer, kt:kt + 1],
                               bias=shift_c[:, layer, kt:kt + 1])
                act.activation(h_full[:, q % 2, k * SEQ:(k + 1) * SEQ], ps, ACT.Identity,
                               scale=scale_c[:, layer, kt:kt + 1],
                               bias=shift_c[:, layer, kt:kt + 1]).then_inc(h_act, 1)

        def q_evac(act, g, end):
            wait(act, s0_done, g)
            qk_evac(act, g, 0, end)

        def qk_evac(act, g, u, end):
            act.wait_ge(granule_used, end)
            for t in range(NT):
                act.activation(qk_in[:, u, t].rearrange("p h d -> p (h d)"), proj[u % 2][t][:], ACT.Copy)
            wait(act, in_evac, 4 * g + u)
            for t in range(NT):
                for h in range(HG):
                    i = (u * NT + t) * HG + h
                    op = act.activation(dump0[:, t, h], proj[u % 2][t][:, h * HD:(h + 1) * HD],
                                        ACT.Square, accum_out=qk_ss[:, i:i + 1])
            op.then_inc(in_evac, 1)

        def copy_evac(act, u, end, dst, func=ACT.Copy, banks=None):
            act.wait_ge(granule_used, end)
            for t in range(NT):
                op = act.activation(dst[:, t, :], (banks or proj[u % 2])[t][:], func)
            op.then_inc(in_evac, 1)

        def qkT_evac(act, g):
            act.wait_ge(qkt_done, g + 1)
            for h in range(HG):
                op = act.activation(qkT[:, h].rearrange("p s t -> p (s t)"), mix[h][:], ACT.Copy)
            op.then_inc(qkT_ready, 1)

        def exp0(act, g):
            act.wait_ge(max_step, 2 * g + 2)
            for h in range(HG):
                for t in range(NT):
                    a, b = (0, P) if t == 0 else (P, 3 * P)
                    i = t * HG + h
                    op = act.activation(p0[:, h, a:b], mix[h][:, a:b], ACT.Exp, scale=q_scale[:, i:i + 1],
                                        bias=neg_max[:, i:i + 1], accum_out=row_sum[:, i:i + 1])
            op.then_inc(p0_ready, 1)

        def pT0_evac(act, g):
            act.wait_ge(pt0_done, g + 1)
            for h in range(HG):
                op = act.activation(pT0[:, h, :], mix[h][:, 0:3 * P], ACT.Copy)
            op.then_inc(pT0_ready, 1)

        def y_hi_act(act, n, scales=None, y_hi=y_hi):
            act.wait_ge(yt_done, n + 1)
            for f in range(4):
                op = act.activation(y_hi[:, f, :], mix[2 + f // 2][:, (f % 2) * SEQ:(f % 2 + 1) * SEQ], ACT.Copy,
                                    **({} if scales is None else {"scale": vnorm_c[:, bass.ds(scales * 4 + f, 1)]}))
            op.then_inc(y_hi_ready, 1)

        def gate_evac(act, bank, b):
            act.wait_ge(gate_summed, b + 1)
            act.activation(gate[:, (b % CHUNKS) * NC:(b % CHUNKS + 1) * NC], mix[bank][:], ACT.Copy
                           ).then_inc(gate_out, 1)

        def act_group0(act, g, it, base):
            def end(u):
                return number(it, base + UNIT * (u + 1))
            tasks = {7: [lambda: q_evac(act, g, end(0))],
                     15: [lambda: qk_evac(act, g, 1, end(1))],
                     20: [lambda: qkT_evac(act, g)],
                     23: [lambda: copy_evac(act, 2, end(2), v0), lambda: exp0(act, g)],
                     27: [lambda: pT0_evac(act, g)],
                     31: [lambda: copy_evac(act, 3, end(3), z0.rearrange("p t h d -> p t (h d)"), ACT.Silu)]}
            return tasks

        def conv_in(act, h, end):
            act.wait_ge(granule_used, end)
            for b in range(2):
                op = act.activation(qk_pad[:, 2 * b:2 * b + 2, TAPS - 1:],
                                    proj[0][b][:].rearrange("p (j t) -> p j t", j=2), ACT.Copy)
            op.then_inc(in_evac, 1)

        def silu_qk(act, h):
            act.wait_ge(conv_step, 16 * h + 16)
            act.activation(cv.rearrange("p j t -> p (j t)"), cv.rearrange("p j t -> p (j t)"), ACT.Silu
                           ).then_inc(qk1_ready, 1)

        def decay1(act, h):
            if isinstance(h, int) and h == 0:
                act.wait_ge(neg_m_ready, 1)
                act.wait_ge(bc_ready, H1)
            for t in range(NT):
                a, b = (0, P) if t == 0 else (P, 3 * P)
                op = act.activation(decay[:, a:b], a_bc_flat[:, bass.ds(h * 384 + a, b - a)], ACT.Exp,
                                    bias=neg_m_flat[:, bass.ds(h + t * H1, 1)])
            op.then_inc(d1_ready, 1)

        def pT1_evac(act, h):
            act.wait_ge(pt1_done, h + 1)
            act.activation(pT1, mix[1][:, 0:3 * P], ACT.Copy).then_inc(pT1_ready, 1)

        def squares1(act, h):
            act.wait_ge(pv1_done, h + 1)
            for t in range(NT):
                op = act.activation(y1[:, t, :], mix[2 + t][:], ACT.Square, accum_out=ss1[:, t:t + 1])
            op.then_inc(sq1_ready, 1)

        def bc_evac(act, heads):
            for h in heads:
                act.wait_ge(bc_done, h + 1)
                act.activation(a_bc[:, h, :], mix[BC_BANK[h % 3]][:, 0:3 * P], ACT.Copy).then_inc(bc_ready, 1)

        def act_group1(act, h, it, base):
            def end(u):
                return number(it, base + UNIT * (u + 1))
            return {7: [lambda: conv_in(act, h, end(0))],
                    12: [lambda: silu_qk(act, h)],
                    14: [lambda: decay1(act, h)],
                    15: [lambda: copy_evac(act, 1, end(1), v1)],
                    17: [lambda: pT1_evac(act, h)],
                    19: [lambda: squares1(act, h)],
                    23: [lambda: copy_evac(act, 2, end(2), o1, ACT.Sigmoid)],
                    31: [lambda: copy_evac(act, 3, end(3), z1, ACT.Silu)]}

        def run(eng, prepare, it, base, n, tasks, start=0):
            for i in range(start, n):
                prepare(eng, it, base + i + LEAD)
                for task in tasks.get(i, []):
                    task()

        def merged(*tables):
            out = {}
            for t in tables:
                for i, tasks in t.items():
                    out.setdefault(i, []).extend(tasks)
            return out

        def gate_tasks(fn, places, b0):
            return {p: [lambda j=j, bank=bank: fn(bank, b0 + j)] for j, (p, bank) in enumerate(places)}

        def act_program(act):
            act.wait_ge(consts_in, 16)
            act.activation(mask_b[:], const[:, C_MASK:C_MASK + P], ACT.Copy)
            act.activation(ident_b[:], ident, ACT.Copy).then_inc(masks_ready, 1)
            act.wait_ge(rows_turned, 1)
            act.activation(cond[:], proj[1][0][:, 0:KT], ACT.Silu).then_inc(cond_ready, 1)
            norm_act(act, 0)
            for b in range(4):
                for i in range(5):
                    hi(act, 0, 6 * b + i)
                h_make(act, 0, 2 * b)
                h_make(act, 0, 2 * b + 1)
                hi(act, 0, 6 * b + 5)
            ends = {19: lambda: q_evac(act, 0, 20), 21: lambda: qk_evac(act, 0, 1, 22),
                    23: lambda: copy_evac(act, 2, 24, v0, banks=mix)}
            for i in range(19, MIXED):
                hi(act, 0, i + LEAD)
                if i in ends:
                    ends[i]()
            z_copy = lambda end: copy_evac(act, 3, end, z0.rearrange("p t h d -> p t (h d)"), ACT.Silu)
            run(act, hi, 0, 0, HEAD, {
                25: [lambda: qkT_evac(act, 0)], 27: [lambda: exp0(act, 0)], 30: [lambda: pT0_evac(act, 0)],
                31: [lambda: z_copy(HEAD)]}, MIXED)
            act.wait_ge(gates_in, 32)
            act.activation(gate_hi[:], gate_w[:], ACT.Copy).then_inc(gate_hi_ready, 1)
            with act.Fori(0, G0 - 2) as it:
                run(act, hi, it, HEAD, BODY, merged(
                    {1: [lambda: y_hi_act(act, it)]}, act_group0(act, it + 1, it, HEAD)))
            it = G0 - 2
            run(act, hi, it, HEAD, BODY, merged(
                {1: [lambda: y_hi_act(act, it)], 34: [lambda: y_hi_act(act, G0 - 1, None, y_hi_last)]},
                act_group0(act, G0 - 1, it, HEAD),
                gate_tasks(lambda bank, b: gate_evac(act, bank, b), SUM_GATE0, 0)))
            run(act, hi, 0, HEAD + (G0 - 1) * BODY, UNIT, {})
            norm_act(act, 1)
            for q in range(4, UNIT):
                h_make(act, 1, q)
            run(act, hi, 0, NG0, HEAD, merged(
                {8: [lambda: gates_exp(act)], 9: [lambda: gates_ln(act)],
                 11: [lambda: floor_exp(act), lambda: bc_evac(act, (0, 1, 2))],
                 12: [lambda: bc_evac(act, (3, 4, 5))], 13: [lambda: bc_evac(act, (6, 7))]},
                act_group1(act, 0, 0, NG0),
                gate_tasks(lambda bank, b: gate_evac(act, bank, b), SUM_GATE1, CHUNKS)))
            with act.Fori(0, H1 - 2) as it:
                run(act, hi, it, NG0 + HEAD, BODY, merged(
                    {1: [lambda: y_hi_act(act, it + G0, it)]}, act_group1(act, it + 1, it, NG0 + HEAD)))
            it = H1 - 2
            run(act, hi, it, NG0 + HEAD, BODY, merged(
                {1: [lambda: y_hi_act(act, it + G0, it)],
                 34: [lambda: y_hi_act(act, G0 + H1 - 1, H1 - 1, y_hi_last)]},
                act_group1(act, H1 - 1, it, NG0 + HEAD)))
            run(act, hi, 0, NG0 + HEAD + (H1 - 1) * BODY, UNIT - LEAD, {})

        def lo(dve, it, c):
            dve.wait_ge(hi_ready, number(it, c) + 1)
            dve.tensor_tensor(w_lo[:, c % LEAD, :], raw[:, c % LEAD, :], w_hi[:, c % LEAD, :].bitcast(F32),
                              ALU.subtract).then_inc(lo_ready, 1)

        def take_ada(dve, it, first, a):
            n = first + a
            dve.wait_ge(ada_in[n % ADA_SLOTS], it * (2 * KT // ADA_SLOTS * 16) + (n // ADA_SLOTS + 1) * 16)
            t, flat = a % KT, "p s n -> p (s n)"
            w, sum_ = ada_raw[:, n % ADA_SLOTS].rearrange(flat), ada_acc[:, a // KT % 2].rearrange(flat)
            if t:
                dve.wait_ge(ada_tile, it * (2 * KT) + n)
                other = sum_
            else:
                if first >= ADA_GATE1:
                    dve.wait_ge(gate_summed, 2 * (a // KT + 1))
                else:
                    wait(dve, ada_summed, it * 2 + (n // KT - 1))
                dve.wait_ge(ada_bias_in, it * 32 + (n // KT + 1) * 16)
                other = ada_bias[:].rearrange(flat)
            dve.scalar_tensor_tensor(out=sum_, in0=w, scalar=cond[:, t:t + 1], in1=other,
                                     op0=ALU.mult, op1=ALU.add).then_inc(ada_tile, 1)

        def ada_tasks(dve, it, first, at):
            return {i: [lambda a=a: take_ada(dve, it, first, a) for a in g] for i, g in at.items()}

        def mod_evac(dve, bank, k, layer, b):
            dve.wait_ge(ada_summed, k + 1)
            at = bass.ds(b * 4 + layer * KT, 4)
            dve.tensor_copy(shift_flat[:, at], mix[bank][:, 0:4])
            dve.scalar_tensor_tensor(out=scale_flat[:, at], in0=mix[bank][:, 4:8], scalar=1.0, in1=norm_c[:, at],
                                     op0=ALU.add, op1=ALU.mult).then_inc(mod_out, 1)

        def norm_sum(dve, layer):
            dve.wait_ge(xsq_ready, NT * CHUNKS * (layer + 1))
            dve.tensor_reduce(xss, xsq, AX.X, ALU.add).then_inc(xss_ready, 1)

        def norm_scale(dve, layer):
            dve.wait_ge(xrs_step, 2 * (layer + 1))
            for q in range(CHUNKS):
                if layer == 1 and q > 1:
                    h_rest(dve, 1, 2 * (q - 2))
                    h_rest(dve, 1, 2 * (q - 2) + 1)
                dve.tensor_scalar(xn[:, 1, q * NC:(q + 1) * NC], stream[:, 1, q * NC:(q + 1) * NC],
                                  xrs[:, 1:2], None, ALU.mult).then_inc(xn_dve, 1)

        def h_rest(dve, layer, q):
            dve.wait_ge(h_act, KT * layer + 2 * (q + 1))
            dve.tensor_tensor(h_lo[:, 2 * q:2 * q + 2, :].rearrange("p k t -> p (k t)"), h_full[:, q % 2, :],
                              h_hi[:, 2 * q:2 * q + 2, :].rearrange("p k t -> p (k t)").bitcast(F32),
                              ALU.subtract).then_inc(h_ready, 1)

        def rope_tables(dve):
            dve.wait_ge(norms_in, 48)
            half = HD // 2
            for i in range(2):
                for t in range(NT):
                    dve.tensor_tensor(rope_a[:, i, t, :], trig[:, 0, t, :], qk_norm[:, i, :], ALU.mult)
                    dve.tensor_tensor(rope_b[:, i, t, 0:half], trig[:, 1, t, 0:half], qk_norm[:, i, half:HD], ALU.mult)
                    op = dve.tensor_tensor(rope_b[:, i, t, half:HD], trig[:, 1, t, half:HD], qk_norm[:, i, 0:half],
                                           ALU.mult)
            op.then_inc(rope_table, 1)

        def rope(dve, g, u):
            half = HD // 2
            dve.wait_ge(in_evac, 4 * g + u + 1)
            wait(dve, rope_done, 2 * g + u)
            if u == 0:
                wait(dve, pv0_done, g)
            src, dst = qk_in[:, u], rot[:, u]
            for t in range(NT):
                dve.tensor_tensor(dst[:, t], src[:, t], rope_a[:, u, t:t + 1, :].to_broadcast([P, HG, HD]), ALU.mult)
                dve.tensor_tensor(swapped[:, t, :, 0:half], src[:, t, :, half:HD],
                                  rope_b[:, u, t:t + 1, 0:half].to_broadcast([P, HG, half]), ALU.mult)
                op = dve.tensor_tensor(swapped[:, t, :, half:HD], src[:, t, :, 0:half],
                                       rope_b[:, u, t:t + 1, half:HD].to_broadcast([P, HG, half]), ALU.mult)
            op.then_inc(rope_part, 1)
            dve.wait_ge(rope_part, 3 * g + 1 + u)
            flat = "p t h d -> p (t h d)"
            op = dve.tensor_tensor(dst.rearrange(flat), dst.rearrange(flat), swapped.rearrange(flat), ALU.add)
            if u == 1:
                op.then_inc(rope_part, 1)
                dve.wait_ge(rope_part, 3 * g + 3)
                dve.wait_ge(qk_rs_step, 3 * g + 3)
                rs = qk_rs[:, 8:16].rearrange("p (n o) -> p n o", o=1).to_broadcast([P, 8, HD])
                op = dve.tensor_tensor(dst.rearrange("p t h d -> p (t h) d"), dst.rearrange("p t h d -> p (t h) d"),
                                       rs, ALU.mult)
            op.then_inc(rope_done, 1)

        def max0(dve, g):
            dve.wait_ge(s0_done, g + 1)
            for h in range(HG):
                for t in range(NT):
                    a, b = (0, P) if t == 0 else (P, 3 * P)
                    dve.reduce_max(row_max[:, t * HG + h:t * HG + h + 1], mix[h][:, a:b], AX.X)
            dve.tensor_scalar(q_scale, qk_rs[:, 0:8], SCALE0, None, ALU.mult).then_inc(max_step, 1)
            dve.wait_ge(max_step, 2 * g + 1)
            dve.scalar_tensor_tensor(out=neg_max, in0=row_max, scalar=-1.0, in1=q_scale,
                                     op0=ALU.mult, op1=ALU.mult).then_inc(max_step, 1)

        def inv0(dve, g):
            dve.wait_ge(p0_ready, g + 1)
            dve.reciprocal(inv_sum, row_sum).then_inc(inv0_ready, 1)

        def y0_out(dve, g):
            dve.wait_ge(pv0_done, g + 1)
            dve.wait_ge(inv0_ready, g + 1)
            dve.wait_ge(in_evac, 4 * g + 4)
            for t in range(NT):
                for h in range(HG):
                    i = t * HG + h
                    op = dve.scalar_tensor_tensor(out=y0[:, t, h * HD:(h + 1) * HD], in0=mix[t][:, h * HD:(h + 1) * HD],
                                                  scalar=inv_sum[:, i:i + 1], in1=z0[:, t, h], op0=ALU.mult,
                                                  op1=ALU.mult)
            op.then_inc(y_done, 1)

        def y_lo_dve(dve, n, scales=None, y_hi=y_hi, y_lo=y_lo):
            dve.wait_ge(y_hi_ready, n + 1)
            for f in range(4):
                src = mix[2 + f // 2][:, (f % 2) * SEQ:(f % 2 + 1) * SEQ]
                if scales is None:
                    op = dve.tensor_tensor(y_lo[:, f, :], src, y_hi[:, f, :].bitcast(F32), ALU.subtract)
                else:
                    op = dve.scalar_tensor_tensor(out=y_lo[:, f, :], in0=src, scalar=vnorm_c[:, bass.ds(scales * 4 + f, 1)],
                                                  in1=y_hi[:, f, :].bitcast(F32), op0=ALU.mult, op1=ALU.subtract)
            op.then_inc(y_lo_ready, 1)

        def out_evac0(dve, o, q, end):
            dve.wait_ge(granule_used, end)
            dve.wait_ge(out_evac, o * CHUNKS + (q + 2))
            for t in range(NT):
                x_t = stream[:, t, q * NC:(q + 1) * NC]
                op = dve.tensor_tensor(x_t, proj[q % 2][t][:], x_t, ALU.add)
            op.then_inc(out_evac, 1)

        def out_evac1(dve, o, q, end):
            dve.wait_ge(granule_used, end)
            dve.wait_ge(out_evac, o * CHUNKS + (q + 2))
            for t in range(NT):
                op = dve.tensor_tensor(scaled[:, t, :], proj[q % 2][t][:], gate[:, q * NC:(q + 1) * NC], ALU.mult)
            op.then_inc(out_part, 1)
            dve.wait_ge(out_part, (o - G0) * CHUNKS + (q + 1))
            for t in range(NT):
                x_t = stream[:, t, q * NC:(q + 1) * NC]
                op = dve.tensor_tensor(x_t, scaled[:, t, :], x_t, ALU.add)
            op.then_inc(out_evac, 1)

        def layer0_end(dve, q):
            dve.wait_ge(out_evac, 2 + CHUNKS * (G0 - 1) + q + 1)
            for t in range(NT):
                x_t = stream[:, t, q * NC:(q + 1) * NC]
                op = dve.tensor_tensor(x_t, x_t, gate[:, q * NC:(q + 1) * NC], ALU.mult)
            op.then_inc(x1_step, 1)
            dve.wait_ge(x1_step, q + 1)
            for t in range(NT):
                x_t = stream[:, t, q * NC:(q + 1) * NC]
                op = dve.tensor_tensor(x_t, x_t, ada_raw[:, q, t, :], ALU.add)
            op.then_inc(x1_chunk, 1)

        def conv(dve, h, tap):
            if tap == 0:
                dve.wait_ge(in_evac, 4 * h + 17)
            for j in range(4):
                w = conv_flat[:, bass.ds(h * (2 * TAPS) + ((j // 2) * (QK1 // P) + j % 2) * TAPS + tap, 1)]
                src = qk_pad[:, j, tap:tap + SEQ]
                if tap == 0:
                    op = dve.tensor_scalar(cv[:, j, :], src, w, None, ALU.mult)
                else:
                    dve.wait_ge(conv_step, h * 16 + (4 * tap + j - 3))
                    op = dve.scalar_tensor_tensor(out=cv[:, j, :], in0=src, scalar=w, in1=cv[:, j, :],
                                                  op0=ALU.mult, op1=ALU.add)
                op.then_inc(conv_step, 1)

        def p1_out(dve, h):
            dve.wait_ge(s1_done, h + 1)
            dve.wait_ge(d1_ready, h + 1)
            for t in range(NT):
                a, b = (0, P) if t == 0 else (P, 3 * P)
                op = dve.scalar_tensor_tensor(out=p1[:, a:b], in0=mix[0][:, a:b], scalar=SCALE1, in1=decay[:, a:b],
                                              op0=ALU.mult, op1=ALU.mult, accum_out=den1[:, t:t + 1])
            op.then_inc(p1_ready, 1)
            dve.wait_ge(p1_ready, h + 1)
            dve.scalar_tensor_tensor(out=inv1, in0=den1, scalar=-1.0, in1=den1, op0=ALU.mult, op1=ALU.max
                                     ).then_inc(den_step, 1)
            dve.wait_ge(den_step, 3 * h + 1)
            if isinstance(h, int) and h == 0:
                dve.wait_ge(floor_ready, 1)
            f = floor_flat[:, :, bass.ds(h, 1)]
            iv = inv1.rearrange("p (t o) -> p t o", o=1)
            dve.tensor_tensor(iv, iv, f, ALU.max).then_inc(den_step, 1)
            dve.wait_ge(den_step, 3 * h + 2)
            dve.reciprocal(inv1, inv1).then_inc(den_step, 1)

        def y1_part(dve, h):
            dve.wait_ge(coef_step, 6 * h + 6)
            dve.wait_ge(in_evac, 4 * h + 19)
            for t in range(NT):
                op = dve.scalar_tensor_tensor(out=y1[:, t, :], in0=mix[2 + t][:], scalar=coef1[:, t:t + 1],
                                              in1=o1[:, t, :], op0=ALU.mult, op1=ALU.mult)
            op.then_inc(y_part, 1)

        def y1_out(dve, h):
            dve.wait_ge(y_part, h + 1)
            dve.wait_ge(in_evac, 4 * h + 20)
            for t in range(NT):
                op = dve.tensor_tensor(y1[:, t, :], y1[:, t, :], z1[:, t, :], ALU.mult)
            op.then_inc(y_done, 1)

        def gates_exp(act):
            act.wait_ge(g_step, 3)
            act.activation(g_b, g_a, ACT.Exp).then_inc(g_act, 1)

        def gates_ln(act):
            act.wait_ge(g_step, 4)
            act.activation(g_a, g_b, ACT.Ln).then_inc(g_act, 1)

        def floor_exp(act):
            act.wait_ge(m_done, 1)
            act.activation(neg_m_flat, mix[2][:, 0:16], ACT.Copy, scale=-1.0).then_inc(neg_m_ready, 1)
            act.activation(floor_m[:].rearrange("p t h -> p (t h)"), mix[2][:, 16:32], ACT.Exp, scale=-1.0
                           ).then_inc(floor_ready, 1)

        def gates_a(dve):
            dve.wait_ge(gates_done, 1)
            for t in range(NT):
                op = dve.tensor_tensor(g_pre[:, t, :], mix[t][:, 0:2 * H1], gate_b[:], ALU.add)
            op.then_inc(g_step, 1)
            dve.wait_ge(g_step, 1)
            dve.tensor_scalar(g_a, g_pre[:, :, H1:], -1.0, None, ALU.mult).then_inc(g_step, 1)
            dve.wait_ge(g_step, 2)
            dve.tensor_tensor(g_a, g_a, g_pre[:, :, H1:], ALU.min).then_inc(g_step, 1)

        def gates_b(dve):
            dve.wait_ge(g_act, 1)
            dve.tensor_scalar(g_b, g_b, 1.0, None, ALU.add).then_inc(g_step, 1)

        def gates_c(dve):
            dve.wait_ge(g_act, 2)
            dve.tensor_scalar(log_f, g_pre[:, :, H1:], 0.0, None, ALU.min).then_inc(g_step, 1)
            dve.wait_ge(g_step, 5)
            dve.tensor_tensor(log_f, log_f, g_a, ALU.subtract).then_inc(g_step, 1)

        def gates_rows(dve):
            dve.wait_ge(cum_done, 1)
            dve.tensor_copy(cum_f, mix[0][0:H1, 0:SEQ]).then_inc(row_step, 1)
            dve.wait_ge(row_step, 1)
            dve.tensor_tensor(a_row, mix[1][0:H1, 0:SEQ], cum_f, ALU.subtract).then_inc(row_step, 1)
            dve.wait_ge(row_step, 2)
            dve.tensor_tensor_scan(out=m_row, data0=a_row, data1=a_row, initial=0.0, op0=ALU.max, op1=ALU.max
                                   ).then_inc(row_step, 1)
            dve.wait_ge(row_step, 3)
            dve.tensor_tensor(m_tot, cum_f, m_row, ALU.add).then_inc(row_step, 1)

        def dve_group0(dve, g, y_at):
            return {8: [lambda: rope(dve, g, 0)], 16: [lambda: rope(dve, g, 1)], 22: [lambda: max0(dve, g)],
                    25: [lambda: inv0(dve, g)], y_at: [lambda: y0_out(dve, g)]}

        def dve_group1(dve, h, y_at):
            return merged({8 + tap: [lambda tap=tap: conv(dve, h, tap)] for tap in range(TAPS)},
                          {14: [lambda: p1_out(dve, h)], 24: [lambda: y1_part(dve, h)], y_at: [lambda: y1_out(dve, h)]})

        def dve_program(dve):
            dve.wait_ge(rows_turned, 1)
            dve.tensor_copy(norm_c[:], proj[0][0][:, 32:64])
            dve.tensor_copy(vnorm_c[:], proj[0][0][:, 64:96])
            dve.tensor_copy(conv_flat, proj[0][1][:, 0:P]).then_inc(rows_out, 1)
            dve.wait_ge(rows_out, 1)
            dve.wait_ge(cond_ready, 1)
            for b in range(5):
                for a in range(KT):
                    if b < 4:
                        take_ada(dve, 0, 0, b * KT + a)
                    if b == 0 and a == 8:
                        norm_sum(dve, 0)
                    if b == 0 and a == 10:
                        norm_scale(dve, 0)
                    if b == 1 and a == 14:
                        rope_tables(dve)
                    if b > 0 and a == 0:
                        mod_evac(dve, 2, b - 1, 0, b - 1)
                    if b > 0 and a in H_STEPS:
                        h_rest(dve, 0, 2 * (b - 1) + H_STEPS.index(a))
                    for i in mixed_at(b, a):
                        lo(dve, 0, i)
            dve.wait_ge(rope_table, 1)
            turned = {20: lambda: rope(dve, 0, 0), 22: lambda: rope(dve, 0, 1)}
            for i in range(19, MIXED):
                lo(dve, 0, i + LEAD)
                if i in turned:
                    turned[i]()
            run(dve, lo, 0, 0, HEAD, {27: [lambda: max0(dve, 0)], 28: [lambda: inv0(dve, 0)],
                                      31: [lambda: y0_out(dve, 0)]}, MIXED)
            dve.wait_ge(gate_hi_ready, 1)
            dve.tensor_tensor(gate_lo[:], gate_w[:], gate_hi[:].bitcast(F32), ALU.subtract).then_inc(gate_lo_ready, 1)
            dve.wait_ge(stream_zeroed, 1)
            def evacs0(it):
                return {HEAD + 2 * q + 1: [lambda q=q: out_evac0(dve, it, q, number(it, HEAD + HEAD + 2 * q + 2))]
                        for q in range(CHUNKS)}
            with dve.Fori(0, G0 - 2) as it:
                run(dve, lo, it, HEAD, BODY, merged(
                    {1: [lambda: y_lo_dve(dve, it)]}, dve_group0(dve, it + 1, 32), evacs0(it),
                    ada_tasks(dve, it, ADA_LOOP, AT_LOOP),
                    {p: [lambda j=j, bank=bank: mod_evac(dve, bank, it * 2 + (4 + j), 1, it * 2 + j)]
                     for j, (p, bank) in enumerate(SUM_LOOP)}))
            it = G0 - 2
            run(dve, lo, it, HEAD, BODY, merged(
                {1: [lambda: y_lo_dve(dve, it)], 34: [lambda: y_lo_dve(dve, G0 - 1, None, y_hi_last, y_lo_last)]},
                dve_group0(dve, it + 1, 32), evacs0(it), ada_tasks(dve, 0, ADA_GATE0, AT_GATE0)))
            dve.wait_ge(gate_out, CHUNKS)
            dve.wait_ge(x_again, 16 * CHUNKS)
            run(dve, lo, 0, HEAD + (G0 - 1) * BODY, UNIT, {
                2 * q + 1: [lambda q=q: out_evac0(dve, G0 - 1, q, HEAD + (G0 - 1) * BODY + 2 * q + 2), lambda q=q: layer0_end(dve, q)]
                for q in range(CHUNKS)})
            norm_sum(dve, 1)
            norm_scale(dve, 1)
            for q in range(4, UNIT):
                h_rest(dve, 1, q)
            dve.wait_ge(pad_zeroed, 1)
            run(dve, lo, 0, NG0, HEAD, merged(
                {7: [lambda: gates_a(dve)], 8: [lambda: gates_b(dve)], 9: [lambda: gates_c(dve)],
                 10: [lambda: gates_rows(dve)]},
                dve_group1(dve, 0, 31), ada_tasks(dve, 0, ADA_GATE1, AT_GATE1)))
            dve.wait_ge(gate_out, 2 * CHUNKS)

            def evacs1(it):
                return {HEAD + 2 * q + 1: [lambda q=q: out_evac1(dve, it + G0, q, number(it, NG0 + HEAD + HEAD + 2 * q + 2))]
                        for q in range(CHUNKS)}
            with dve.Fori(0, H1 - 2) as it:
                run(dve, lo, it, NG0 + HEAD, BODY, merged(
                    {1: [lambda: y_lo_dve(dve, it + G0, it)]}, dve_group1(dve, it + 1, 32), evacs1(it)))
            it = H1 - 2
            run(dve, lo, it, NG0 + HEAD, BODY, merged(
                {1: [lambda: y_lo_dve(dve, it + G0, it)],
                 34: [lambda: y_lo_dve(dve, G0 + H1 - 1, H1 - 1, y_hi_last, y_lo_last)]},
                dve_group1(dve, it + 1, 32), evacs1(it)))
            base = NG0 + HEAD + (H1 - 1) * BODY
            for i in range(UNIT):
                if i < UNIT - LEAD:
                    lo(dve, 0, base + i + LEAD)
                if i % 2:
                    out_evac1(dve, G0 + H1 - 1, i // 2, base + i + 1)

        def gpsimd_program(pool):
            pool.memset(ada_bias[:], 0.0).then_inc(bias_zeroed, 1)
            pool.memset(ones[:], 1.0).then_inc(ones_set, 1)
            pool.memset(eps_c[:], EPS)
            pool.memset(per_hd[:], 1.0 / HD)
            pool.memset(per_dv[:], 1.0 / DV)
            pool.memset(neg_half[:], -0.5).then_inc(half_set, 1)
            pool.memset(qk_pad[:, :, 0:TAPS - 1], 0.0).then_inc(pad_zeroed, 1)
            pool.wait_ge(half_set, 1)

            def norm_power(layer):
                pool.wait_ge(xss_ready, layer + 1)
                pool.tensor_scalar(xrs, xss, 1.0 / D, EPS, ALU.mult, ALU.add).then_inc(xrs_step, 1)
                pool.wait_ge(xrs_step, 2 * layer + 1)
                pool.tensor_tensor(xrs, xrs, neg_half[:, 0:2], ALU.pow).then_inc(xrs_step, 1)

            norm_power(0)
            pool.wait_ge(xn_act, CHUNKS)
            pool.wait_ge(xn_dve, CHUNKS)
            pool.memset(stream[:, 0, :], 0.0)
            pool.memset(stream[:, 1, :], 0.0).then_inc(out_evac, 2)
            pool.wait_ge(out_evac, 2)
            pool.sem_inc(stream_zeroed, 1)
            with pool.Fori(0, G0) as g:
                pool.wait_ge(in_evac, 4 * g + 2)
                pool.tensor_tensor(qk_rs, qk_ss, per_hd[:], ALU.mult).then_inc(qk_rs_step, 1)
                pool.wait_ge(qk_rs_step, 3 * g + 1)
                pool.tensor_tensor(qk_rs, qk_rs, eps_c[:], ALU.add).then_inc(qk_rs_step, 1)
                pool.wait_ge(qk_rs_step, 3 * g + 2)
                pool.tensor_tensor(qk_rs, qk_rs, neg_half[:, 0:16], ALU.pow).then_inc(qk_rs_step, 1)
            norm_power(1)
            with pool.Fori(0, H1) as h:
                pool.wait_ge(sq1_ready, h + 1)
                pool.wait_ge(den_step, 3 * h + 3)
                pool.tensor_tensor(t1, inv1, inv1, ALU.mult).then_inc(coef_step, 1)
                for n, (operand, op) in enumerate(((ss1, ALU.mult), (per_dv[:], ALU.mult),
                                                   (eps_c[:, 0:NT], ALU.add), (neg_half[:, 0:NT], ALU.pow))):
                    pool.wait_ge(coef_step, 6 * h + (n + 1))
                    pool.tensor_tensor(t1, t1, operand, op).then_inc(coef_step, 1)
                pool.wait_ge(coef_step, 6 * h + 5)
                pool.tensor_tensor(coef1, t1, inv1, ALU.mult).then_inc(coef_step, 1)

        def slot(w, c, k):
            return w[:, c % LEAD, k * NC:(k + 1) * NC]

        def three(pe, out_, a_hi, a_lo, b_hi, b_lo, start, stop, **kw):
            pe.matmul(out_, a_hi, b_hi, start=start, stop=False, **kw)
            pe.matmul(out_, a_hi, b_lo, start=False, stop=False, **kw)
            return pe.matmul(out_, a_lo, b_hi, start=False, stop=stop, **kw)

        def unit_wait(pe, n, u, o):
            wait(pe, in_evac, n - 1)
            if u < 2:
                pe.wait_ge(out_evac, o * CHUNKS + (1 + u))

        def granule_in(pe, it, c, u, r, banks=None):
            pe.wait_ge(lo_ready, number(it, c) + 1)
            for k in range(KG):
                kt = KG * r + k
                for t in range(NT):
                    a, b = h_hi[:, kt, t * P:(t + 1) * P], h_lo[:, kt, t * P:(t + 1) * P]
                    op = three(pe, (banks or proj[u % 2])[t][:], a, b, slot(w_hi, c, k), slot(w_lo, c, k),
                               kt == 0, kt == KT - 1)
            op.then_inc(granule_used, 1)

        def granule_qk1(pe, it, c, r):
            pe.wait_ge(lo_ready, number(it, c) + 1)
            for k in range(2 * KG):
                kt = 2 * KG * (r % 4) + k
                for j in range(2):
                    w = slice(k * DK + j * P, k * DK + (j + 1) * P)
                    op = three(pe, proj[0][r // 4][:, j * SEQ:(j + 1) * SEQ], w_hi[:, c % LEAD, w],
                               w_lo[:, c % LEAD, w], h_hi[:, kt, :], h_lo[:, kt, :],
                               kt == 0 and j == 0, kt == KT - 1, skip_group_check=True)
            op.then_inc(granule_used, 1)

        def granule_out(pe, o, it, c, q, n=None, y_hi=y_hi, y_lo=y_lo):
            j = q // 2
            pe.wait_ge(lo_ready, number(it, c) + 1)
            if q == 0:
                pe.wait_ge(y_lo_ready, o + 1)
            if q % 2 == 0:
                if j < 2 and n is not None:
                    pe.wait_ge(in_evac, n - 1 + j)
                else:
                    pe.wait_ge(out_evac, o * CHUNKS + (j + 1))
            for k in range(KG):
                f = KG * (q % 2) + k
                for t in range(NT):
                    a, b = y_hi[:, f, t * P:(t + 1) * P], y_lo[:, f, t * P:(t + 1) * P]
                    op = three(pe, proj[j % 2][t][:], a, b, slot(w_hi, c, k), slot(w_lo, c, k), f == 0, f == 3)
            op.then_inc(granule_used, 1)

        def turn_rows(pe):
            pe.wait_ge(consts_in, 16)
            pe.wait_ge(rows_in, 64)
            pe.transpose(proj[1][0][:, 0:KT], rows_c, ident[0:KT, 0:KT])
            pe.transpose(proj[0][0][:, 32:64], rows_n, ident[0:32, 0:32])
            pe.transpose(proj[0][0][:, 64:96], rows_v, ident[0:32, 0:32])
            for j in range(2 * QK1 // P):
                op = pe.transpose(proj[0][1][:, j * TAPS:(j + 1) * TAPS], conv_rows[:, j * P:(j + 1) * P],
                                  ident[0:TAPS, 0:TAPS])
            op.then_inc(rows_turned, 1)

        def turn_x(pe, layer, q):
            pe.wait_ge(xn_act, CHUNKS * layer + q // 2 + 1)
            pe.wait_ge(xn_dve, CHUNKS * layer + q // 2 + 1)
            before = q - (4 if layer else 2)
            if before >= 0:
                pe.wait_ge(h_act, KT * layer + 2 * (before + 1))
            for k in range(2):
                for t in range(NT):
                    kt = 2 * q + k
                    op = pe.transpose(turn_bank(layer, q)[:, k * SEQ + t * P:k * SEQ + (t + 1) * P],
                                      xn[:, t, kt * P:(kt + 1) * P], ident)
            op.then_inc(ht_done, 1)

        def mod_sum(pe, bank, k, which):
            pe.wait_ge(ada_tile, k * KT + KT)
            for j in range(8):
                op = pe.matmul(mix[bank][:, j:j + 1], ada_acc[:, which, j // 4, j % 4 * P:(j % 4 + 1) * P],
                               ones[:, 0:1], start=True, stop=True)
            op.then_inc(ada_summed, 1)

        def gate_sum(pe, bank, b):
            first = (ADA_GATE0 if b < CHUNKS else ADA_GATE1) // KT
            pe.wait_ge(ada_tile, (first + b % CHUNKS // 2 + 1) * KT)
            op = pe.matmul(mix[bank][:], ones[:], ada_acc[:, b // 2 % 2, b % 2, :], start=True, stop=True)
            op.then_inc(gate_summed, 1)

        def turn_qk0(pe, g, free, count):
            pe.wait_ge(rope_done, 2 * g + 2)
            wait(pe, y_lo_ready, g)
            pe.wait_ge(free, count)
            for h in range(HG):
                for u in range(2):
                    for t in range(NT):
                        op = pe.transpose(mix[h][:, (u * NT + t) * P:(u * NT + t + 1) * P], rot[:, u, t, h, :], ident)
            op.then_inc(qkt_done, 1)

        def masked(pe, bank):
            return pe.matmul(bank, ident_b[:], mask_b[:], start=False, stop=True)

        def scores0(pe, g):
            pe.wait_ge(qkT_ready, g + 1)
            for h in range(HG):
                q, k = qkT[:, h, 0, :], qkT[:, h, 1, :]
                pe.matmul(mix[h][:, 0:P], q[:, 0:P], k[:, 0:P], start=True, stop=False)
                masked(pe, mix[h][:, 0:P])
                pe.matmul(mix[h][:, P:3 * P], q[:, P:SEQ], k, start=True, stop=False, skip_group_check=True)
                op = pe.matmul(mix[h][:, 2 * P:3 * P], ident_b[:], mask_b[:], start=False, stop=True,
                               skip_group_check=True)
            op.then_inc(s0_done, 1)

        def turn_p0(pe, g):
            pe.wait_ge(p0_ready, g + 1)
            for h in range(HG):
                for i in range(3):
                    op = pe.transpose(mix[h][:, i * P:(i + 1) * P], p0[:, h, i * P:(i + 1) * P], ident)
            op.then_inc(pt0_done, 1)

        def pv0(pe, g):
            pe.wait_ge(pT0_ready, g + 1)
            pe.wait_ge(in_evac, 4 * g + 3)
            for h in range(HG):
                d = slice(h * HD, (h + 1) * HD)
                pe.matmul(mix[0][:, d], pT0[:, h, 0:P], v0[:, 0, d], start=True, stop=True)
                pe.matmul(mix[1][:, d], pT0[:, h, P:2 * P], v0[:, 0, d], start=True, stop=False)
                op = pe.matmul(mix[1][:, d], pT0[:, h, 2 * P:3 * P], v0[:, 1, d], start=False, stop=True)
            op.then_inc(pv0_done, 1)

        def turn_y(pe, n, y, mods=None):
            if mods is not None:
                pe.wait_ge(mod_out, mods)
            pe.wait_ge(y_done, n + 1)
            for f in range(4):
                for t in range(NT):
                    op = pe.transpose(mix[2 + f // 2][:, (f % 2) * SEQ + t * P:(f % 2) * SEQ + (t + 1) * P],
                                      y[:, t, f * P:(f + 1) * P], ident)
            op.then_inc(yt_done, 1)

        def pe_group0(pe, g, free, count):
            return {20: [lambda: turn_qk0(pe, g, free, count)], 22: [lambda: scores0(pe, g)],
                    27: [lambda: turn_p0(pe, g)], 31: [lambda: pv0(pe, g)]}

        def sum_behind(pe, bank_sem, count, sum_, *args):
            pe.wait_ge(bank_sem, count)
            sum_(pe, *args)

        def gates1(pe):
            pe.wait_ge(gate_lo_ready, 1)
            for t in range(NT):
                for kt in range(KT):
                    op = three(pe, mix[t][:, 0:2 * H1], h_hi[:, kt, t * P:(t + 1) * P], h_lo[:, kt, t * P:(t + 1) * P],
                               gate_hi[:, kt, :], gate_lo[:, kt, :], kt == 0, kt == KT - 1)
            op.then_inc(gates_done, 1)

        def gates_cum(pe):
            pe.wait_ge(g_step, 6)
            pe.matmul(mix[0][0:H1, 0:SEQ], log_f[:, 0, :], tri[:, 0:SEQ], start=True, stop=False,
                      skip_group_check=True)
            pe.matmul(mix[0][0:H1, P:SEQ], log_f[:, 1, :], tri[:, 0:P], start=False, stop=True,
                      skip_group_check=True)
            for t in range(NT):
                op = pe.transpose(mix[1][0:H1, t * P:(t + 1) * P], g_pre[:, t, 0:H1], ident)
            op.then_inc(cum_done, 1)

        def turn_m(pe):
            pe.wait_ge(row_step, 4)
            for i, row in enumerate((m_row, m_tot)):
                for t in range(NT):
                    op = pe.transpose(mix[2][:, (i * NT + t) * H1:(i * NT + t + 1) * H1],
                                      row[:, t * P:(t + 1) * P], ident[0:H1, 0:H1])
            op.then_inc(m_done, 1)

        def broadcast_a(pe, heads, before):
            wait(pe, bc_ready, before)
            for h in heads:
                bank = mix[BC_BANK[h % 3]]
                one = ident[0:H1, h:h + 1].to_broadcast([H1, P])
                pe.matmul(bank[:, 0:P], one, a_row[:, 0:P], start=True, stop=False)
                masked(pe, bank[:, 0:P])
                pe.matmul(bank[:, P:3 * P], one, a_row, start=True, stop=False, skip_group_check=True)
                pe.matmul(bank[:, 2 * P:3 * P], ident_b[:], mask_b[:], start=False, stop=True,
                          skip_group_check=True).then_inc(bc_done, 1)

        def scores1(pe, h):
            pe.wait_ge(qk1_ready, h + 1)
            if isinstance(h, int) and h == 0:
                pe.wait_ge(bc_ready, H1)
            else:
                pe.wait_ge(p1_ready, h)
            for a, b, q in ((0, P, slice(0, P)), (P, 3 * P, slice(P, SEQ))):
                for j in range(2):
                    op = pe.matmul(mix[0][:, a:b], cv[:, j, q], cv[:, 2 + j, 0:b - a], start=(j == 0), stop=(j == 1))
            op.then_inc(s1_done, 1)

        def turn_p1(pe, h):
            pe.wait_ge(p1_ready, h + 1)
            for i in range(3):
                op = pe.transpose(mix[1][:, i * P:(i + 1) * P], p1[:, i * P:(i + 1) * P], ident)
            op.then_inc(pt1_done, 1)

        def pv1(pe, h):
            pe.wait_ge(pT1_ready, h + 1)
            pe.wait_ge(in_evac, 4 * h + 18)
            pe.wait_ge(y_lo_ready, h + G0)
            if isinstance(h, int) and h == 0:
                pe.wait_ge(gate_out, CHUNKS + 2)
            pe.matmul(mix[2][:], pT1[:, 0:P], v1[:, 0, :], start=True, stop=True)
            pe.matmul(mix[3][:], pT1[:, P:2 * P], v1[:, 0, :], start=True, stop=False)
            pe.matmul(mix[3][:], pT1[:, 2 * P:3 * P], v1[:, 1, :], start=False, stop=True).then_inc(pv1_done, 1)

        def pe_group1(pe, h):
            return {14: [lambda: scores1(pe, h)], 17: [lambda: turn_p1(pe, h)], 19: [lambda: pv1(pe, h)]}

        def pe_segment(pe, it, base, layer, group, o, tasks, out_too, before=None):
            for i in range(BODY if out_too else HEAD):
                u, r = i // UNIT, i % UNIT
                if u < 4 and r == 0:
                    unit_wait(pe, group * 4 + (4 * G0 * layer + u), u, o)
                if before and u == 0:
                    before(i)
                if u == 4:
                    granule_out(pe, o, it, base + i, r, group * 4 + (4 * G0 * layer + 4))
                elif u == 0 and layer == 1:
                    granule_qk1(pe, it, base + i, r)
                else:
                    granule_in(pe, it, base + i, u, r)
                for task in tasks.get(i, []):
                    task()

        def pe_program(pe):
            turn_rows(pe)
            pe.wait_ge(ones_set, 1)
            pe.wait_ge(rows_out, 1)
            pe.wait_ge(masks_ready, 1)
            for b in range(4):
                turn_x(pe, 0, 2 * b)
                wait(pe, h_act, 4 * b)
                mod_sum(pe, 2, b, b % 2)
                pe.wait_ge(mod_out, b + 1)
                turn_x(pe, 0, 2 * b + 1)
                for i in range(6 * b, 6 * b + 6):
                    u, r = head0(i)
                    pe.wait_ge(h_ready, r + 1)
                    granule_in(pe, 0, i, u, r, mix if u == 2 else None)
            tasks = {25: [lambda: turn_qk0(pe, 0, in_evac, 3)], 27: [lambda: scores0(pe, 0)],
                     30: [lambda: turn_p0(pe, 0)], 31: [lambda: pv0(pe, 0)]}
            unit_wait(pe, 3, 3, 0)
            for i in range(MIXED, HEAD):
                granule_in(pe, 0, i, 3, i - MIXED)
                for task in tasks.get(i, []):
                    task()
            with pe.Fori(0, G0 - 2) as it:
                (p0_at, b0), (p1_at, b1) = SUM_LOOP
                pe_segment(pe, it, HEAD, 0, it + 1, it, merged(
                    {1: [lambda: turn_y(pe, it, y0, 2 * it + 4)],
                     p0_at: [lambda: sum_behind(pe, y_lo_ready, it + 1, mod_sum, b0, it * 2 + 4, 0)],
                     p1_at: [lambda: sum_behind(pe, pT0_ready, it + 2, mod_sum, b1, it * 2 + 5, 1)]},
                    pe_group0(pe, it + 1, mod_out, it * 2 + 5)), True)
            it = G0 - 2
            free = [(y_lo_ready, it + 1)] * 2 + [(y_lo_ready, G0)] * 2
            pe_segment(pe, it, HEAD, 0, it + 1, it, merged(
                {1: [lambda: turn_y(pe, it, y0, 2 * CHUNKS)], 34: [lambda: turn_y(pe, G0 - 1, y0)]},
                pe_group0(pe, it + 1, gate_out, 2),
                gate_tasks(lambda bank, b: sum_behind(pe, *free[b], gate_sum, bank, b), SUM_GATE0, 0)), True)
            for q in range(UNIT):
                granule_out(pe, G0 - 1, 0, HEAD + (G0 - 1) * BODY + q, q, None, y_hi_last, y_lo_last)
            pe.wait_ge(gate_out, CHUNKS)

            def rest_of_h(i):
                for q in {1: [4, 5], 2: [6, 7]}.get(i, []):
                    turn_x(pe, 1, q)
                pe.wait_ge(h_ready, UNIT + min(UNIT, 2 * (i + 1)))

            for q in range(4):
                turn_x(pe, 1, q)
            free = [(bc_ready, H1), (gate_out, CHUNKS + 1), (p1_ready, 1), (pT1_ready, 1)]
            pe_segment(pe, 0, NG0, 1, 0, G0, merged(
                {7: [lambda: gates1(pe)], 10: [lambda: gates_cum(pe)],
                 11: [lambda: turn_m(pe), lambda: broadcast_a(pe, (0, 1, 2), 0)],
                 12: [lambda: broadcast_a(pe, (3, 4, 5), 3)], 13: [lambda: broadcast_a(pe, (6, 7), 6)]},
                pe_group1(pe, 0),
                gate_tasks(lambda bank, b: sum_behind(pe, *free[b - CHUNKS], gate_sum, bank, b),
                           SUM_GATE1, CHUNKS)), False, rest_of_h)
            pe.wait_ge(gate_out, 2 * CHUNKS)
            with pe.Fori(0, H1 - 2) as it:
                pe_segment(pe, it, NG0 + HEAD, 1, it + 1, it + G0, merged(
                    {1: [lambda: turn_y(pe, it + G0, y1)]}, pe_group1(pe, it + 1)), True)
            it = H1 - 2
            pe_segment(pe, it, NG0 + HEAD, 1, it + 1, it + G0, merged(
                {1: [lambda: turn_y(pe, it + G0, y1)], 34: [lambda: turn_y(pe, G0 + H1 - 1, y1)]},
                pe_group1(pe, it + 1)), True)
            for q in range(UNIT):
                granule_out(pe, G0 + H1 - 1, 0, NG0 + HEAD + (H1 - 1) * BODY + q, q, None,
                            y_hi_last, y_lo_last)

        block = ctx.enter_context(nc.Block())

        @block.sync
        def _(sp):
            sp_program(sp)

        @block.scalar
        def _(act):
            act_program(act)

        @block.vector
        def _(dve):
            dve_program(dve)

        @block.gpsimd
        def _(pool):
            gpsimd_program(pool)

        @block.tensor
        def _(pe):
            pe_program(pe)


_INS = ["x", "c", "norm_w", "ada_w", "ada_b", "att_w_in", "att_q_norm", "att_k_norm", "att_w_out",
        "mlstm_w_in", "mlstm_gate_b", "mlstm_conv_w", "mlstm_norm_w", "mlstm_w_out"]


def _constants():
    import numpy as np
    out = np.zeros((P, C_ALL), np.float32)
    out[:, C_ID:C_ID + P] = np.eye(P)
    out[:, C_TRI:C_TRI + P] = np.triu(np.ones((P, P)))
    out[:, C_TRI + P:C_TRI + 2 * P] = 1.0
    out[:, C_MASK:C_MASK + P] = np.triu(np.full((P, P), MASKED), 1)
    half = HD // 2
    inv = np.float32(10000.0) ** (-np.arange(half, dtype=np.float32) / np.float32(half))
    ang = np.arange(SEQ, dtype=np.float32)[:, None] * inv[None, :]
    cos, sin = np.cos(ang), np.sin(ang)
    for t in range(NT):
        rows = slice(t * P, (t + 1) * P)
        out[:, C_COS + t * HD:C_COS + (t + 1) * HD] = np.concatenate([cos[rows], cos[rows]], 1)
        out[:, C_SIN + t * HD:C_SIN + (t + 1) * HD] = np.concatenate([-sin[rows], sin[rows]], 1)
    return out


def kernel(**inputs):
    import numpy as np
    import concourse.bacc as bacc
    from concourse.bass_utils import run_bass_kernel_spmd

    nc = bacc.Bacc("TRN2", target_bir_lowering=False, num_devices=1)
    arrays = {f"in_{n}": np.ascontiguousarray(inputs[n]) for n in _INS}
    arrays["in_consts"] = _constants()
    args = [nc.dram_tensor(n, a.shape, mybir.dt.from_np(a.dtype), kind="ExternalInput").ap()
            for n, a in arrays.items()]
    out = nc.dram_tensor("out_0", (1, SEQ, D), F32, kind="ExternalOutput").ap()
    build(nc, *args, out)
    r = run_bass_kernel_spmd(nc, [arrays], core_ids=[0])
    return r.results[0]["out_0"]
```
